# Optimizing a Trainium2 kernel written in Bass

```python
import jax
import jax.numpy as jnp
from jax import lax
import numpy as np

D_MODEL = 1024
BATCH = 1
SEQ = 512
DEPTH = 1

EPS = 1e-6
HG_HEADS = 4
HG_DK = 128
HG_DV = 128
HG_QF = HG_HEADS * HG_DK
HG_WIDTH = HG_HEADS * HG_DV
HG_CHUNK = 64
SSM_HEADS = 8
SSM_HEAD_DIM = 64
SSM_WIDTH = SSM_HEADS * SSM_HEAD_DIM
SSM_GROUPS = 2
SSM_STATE = 128
SSM_CONV = 4
SSM_CONV_CH = SSM_WIDTH + 2 * SSM_GROUPS * SSM_STATE
SSM_CHUNK = 128
DT_MIN = 1e-3
DT_MAX = 1e-1
D_MIX = HG_WIDTH + SSM_WIDTH
IN_SPLITS = (HG_QF, HG_QF, HG_WIDTH, HG_WIDTH, SSM_WIDTH, SSM_CONV_CH, SSM_HEADS)
IN_COLS = sum(IN_SPLITS)
N_EXPERTS = 32
TOP_K = 4
D_FF = 1024
SWIGLU_LIMIT = 7.0
SWIGLU_ALPHA = 1.702
MOE_BLOCK = 128
N_MOD = 6

kernel_name = "hgrn2_mamba2_parallel_moe_adaln"

def rmsnorm(x, w):
    xf = x.astype(jnp.float32)
    y = xf * lax.rsqrt(jnp.mean(xf * xf, axis=-1, keepdims=True) + EPS)
    return (y * w.astype(jnp.float32)).astype(x.dtype)

def modulate(h, shift, scale):
    return h * (1.0 + scale[:, None, :]) + shift[:, None, :]

def scan_chunk_states(decay, d_state):
    def step(s, inp):
        dec, ds = inp
        return dec * s + ds, s
    s0 = jnp.zeros_like(d_state[:, 0])
    _, prev = lax.scan(step, s0, (jnp.moveaxis(decay, 1, 0), jnp.moveaxis(d_state, 1, 0)))
    return jnp.moveaxis(prev, 0, 1)

def hgrn2_chunked(q, k, v, log_f):
    bsz, seqlen, nh, _ = q.shape
    c = HG_CHUNK
    n = seqlen // c
    r = lambda t: t.reshape(bsz, n, c, nh, t.shape[-1])
    q, k, v, log_f = r(q), r(k), r(v), r(log_f)
    b = jnp.cumsum(log_f, axis=2)
    b_mid = b[:, :, c // 2 - 1:c // 2]
    b_last = b[:, :, -1]
    causal = jnp.tril(jnp.ones((c, c), dtype=bool))
    att = jnp.einsum('bnthk,bnshk->bnhts', q * jnp.exp(b - b_mid), k * jnp.exp(b_mid - b))
    att = jnp.where(causal, att, 0.0)
    o_intra = jnp.einsum('bnhts,bnshv->bnthv', att, v)
    d_state = jnp.einsum('bnshk,bnshv->bnhkv', k * jnp.exp(b_last[:, :, None] - b), v)
    s_prev = scan_chunk_states(jnp.exp(b_last)[..., None], d_state)
    o_inter = jnp.einsum('bnthk,bnhkv->bnthv', q * jnp.exp(b), s_prev)
    return (o_intra + o_inter).reshape(bsz, seqlen, nh, v.shape[-1])

def ssd_chunked(x, dt, a, bm, cm):
    bsz, seqlen, nh, p = x.shape
    g = bm.shape[2]
    hg = nh // g
    c = SSM_CHUNK
    n = seqlen // c
    x = x.reshape(bsz, n, c, g, hg, p)
    dt = dt.reshape(bsz, n, c, g, hg)
    bm = bm.reshape(bsz, n, c, g, -1)
    cm = cm.reshape(bsz, n, c, g, -1)
    a_cum = jnp.cumsum(dt * a.reshape(g, hg), axis=2)
    a_last = a_cum[:, :, -1]
    xdt = x * dt[..., None]
    a_t = jnp.moveaxis(a_cum, 2, -1)
    causal = jnp.tril(jnp.ones((c, c), dtype=bool))
    seg = jnp.exp(jnp.where(causal, a_t[..., :, None] - a_t[..., None, :], -jnp.inf))
    cb = jnp.einsum('bntgd,bnsgd->bngts', cm, bm)
    scores = cb[:, :, :, None] * seg
    y_intra = jnp.einsum('bnghts,bnsghp->bntghp', scores, xdt)
    d_state = jnp.einsum('bnsgd,bnsgh,bnsghp->bnghpd', bm, jnp.exp(a_last[:, :, None] - a_cum), xdt)
    s_prev = scan_chunk_states(jnp.exp(a_last)[..., None, None], d_state)
    y_inter = jnp.einsum('bntgd,bntgh,bnghpd->bntghp', cm, jnp.exp(a_cum), s_prev)
    return (y_intra + y_inter).reshape(bsz, seqlen, nh, p)

def causal_depthwise_conv(x, w, b):
    y = lax.conv_general_dilated(x, w[:, None, :], window_strides=(1,), padding=[(SSM_CONV - 1, 0)],
                                 dimension_numbers=('NWC', 'WIO', 'NWC'), feature_group_count=x.shape[-1])
    return y + b

def hybrid_mixer(u, w_in, lb, hg_norm_w, a_log, dt_bias, d_skip, conv_w, conv_b, ssm_norm_w, w_out):
    bsz, seqlen, _ = u.shape
    f32 = jnp.float32
    proj = u @ w_in
    q, f, i, g, z, xbc, dt_raw = jnp.split(proj, np.cumsum(IN_SPLITS[:-1]).tolist(), axis=-1)
    hd = lambda t, d: t.reshape(bsz, seqlen, HG_HEADS, d)
    fg = lb + (1.0 - lb) * jax.nn.sigmoid(f.astype(f32))
    o_hg = hgrn2_chunked(hd(jax.nn.silu(q.astype(f32)), HG_DK), hd(1.0 - fg, HG_DK),
                         hd(i.astype(f32), HG_DV), hd(jnp.log(fg), HG_DK))
    o_hg = rmsnorm(o_hg, hg_norm_w) * jax.nn.silu(hd(g.astype(f32), HG_DV))
    o_hg = o_hg.reshape(bsz, seqlen, HG_WIDTH)
    xbc = jax.nn.silu(causal_depthwise_conv(xbc, conv_w, conv_b)).astype(f32)
    xs, bm, cm = jnp.split(xbc, [SSM_WIDTH, SSM_WIDTH + SSM_GROUPS * SSM_STATE], axis=-1)
    xs = xs.reshape(bsz, seqlen, SSM_HEADS, SSM_HEAD_DIM)
    dt = jax.nn.softplus(dt_raw.astype(f32) + dt_bias.astype(f32))
    a = -jnp.exp(a_log.astype(f32))
    y = ssd_chunked(xs, dt, a, bm.reshape(bsz, seqlen, SSM_GROUPS, SSM_STATE),
                    cm.reshape(bsz, seqlen, SSM_GROUPS, SSM_STATE))
    y = y + d_skip.astype(f32)[:, None] * xs
    y = y.reshape(bsz, seqlen, SSM_WIDTH) * jax.nn.silu(z.astype(f32))
    y = rmsnorm(y.reshape(bsz, seqlen, SSM_GROUPS, SSM_WIDTH // SSM_GROUPS),
                ssm_norm_w.reshape(SSM_GROUPS, SSM_WIDTH // SSM_GROUPS)).reshape(bsz, seqlen, SSM_WIDTH)
    mixed = jnp.concatenate([o_hg, y], axis=-1).astype(u.dtype)
    return mixed @ w_out

def moe_ffn(h, router_w, router_b, w1, b1, w2, b2):
    bsz, seqlen, d = h.shape
    t = bsz * seqlen
    n_assign = t * TOP_K
    hf = h.reshape(t, d)
    logits = (hf @ router_w).astype(jnp.float32) + router_b.astype(jnp.float32)
    top_logits, top_idx = lax.top_k(logits, TOP_K)
    gates = jax.nn.softmax(top_logits, axis=-1)
    flat_e = top_idx.reshape(n_assign)
    order = jnp.argsort(flat_e).astype(jnp.int32)
    sorted_e = flat_e[order]
    counts = jnp.bincount(flat_e, length=N_EXPERTS)
    padded = (counts + MOE_BLOCK - 1) // MOE_BLOCK * MOE_BLOCK
    start = jnp.cumsum(counts) - counts
    pend = jnp.cumsum(padded)
    pstart = pend - padded
    dest = pstart[sorted_e] + jnp.arange(n_assign, dtype=jnp.int32) - start[sorted_e]
    n_rows = (n_assign + MOE_BLOCK - 1) // MOE_BLOCK * MOE_BLOCK + N_EXPERTS * MOE_BLOCK
    n_blocks = n_rows // MOE_BLOCK
    row_assign = jnp.full((n_rows,), n_assign, jnp.int32).at[dest].set(order)
    row_tok = row_assign // TOP_K
    block_e = jnp.minimum(jnp.searchsorted(pend, jnp.arange(n_blocks) * MOE_BLOCK, side='right'),
                          N_EXPERTS - 1)
    h_pad = jnp.concatenate([hf, jnp.zeros((1, d), hf.dtype)], axis=0)
    xin = h_pad[row_tok].reshape(n_blocks, MOE_BLOCK, d)

    def expert_block(args):
        xb, e = args
        hb = xb @ w1[e] + b1[e]
        glu, lin = jnp.split(hb, 2, axis=-1)
        glu = jnp.minimum(glu, SWIGLU_LIMIT)
        lin = jnp.clip(lin, -SWIGLU_LIMIT, SWIGLU_LIMIT)
        act = glu * jax.nn.sigmoid(SWIGLU_ALPHA * glu) * (lin + 1.0)
        return act @ w2[e] + b2[e]

    yout = lax.map(expert_block, (xin, block_e)).reshape(n_rows, d)
    gate_rows = jnp.concatenate([gates.reshape(n_assign), jnp.zeros((1,), gates.dtype)])[row_assign]
    out = jax.ops.segment_sum(yout * gate_rows[:, None].astype(yout.dtype), row_tok, num_segments=t + 1)[:t]
    return out.reshape(bsz, seqlen, d)

def setup_inputs(seed: int = 0) -> dict:
    key = jax.random.key(seed)
    ks = jax.random.split(key, 24)
    nrm = lambda k, shape, s: jax.random.normal(k, shape, jnp.float32) * s
    dt0 = jnp.exp(jax.random.uniform(ks[9], (DEPTH, SSM_HEADS), jnp.float32,
                                     jnp.log(DT_MIN), jnp.log(DT_MAX)))
    return {
        'x': nrm(ks[0], (BATCH, SEQ, D_MODEL), 1.0),
        'c': nrm(ks[1], (BATCH, D_MODEL), 1.0),
        'ada_w': nrm(ks[2], (DEPTH, D_MODEL, N_MOD * D_MODEL), 0.5 * D_MODEL ** -0.5),
        'ada_b': nrm(ks[3], (DEPTH, N_MOD * D_MODEL), 0.02),
        'norm1_w': 1.0 + nrm(ks[4], (DEPTH, D_MODEL), 0.02),
        'w_in': nrm(ks[5], (DEPTH, D_MODEL, IN_COLS), D_MODEL ** -0.5),
        'hg_lb_logits': nrm(ks[6], (DEPTH + 1, HG_QF), 0.1),
        'hg_norm_w': 1.0 + nrm(ks[7], (DEPTH, HG_DV), 0.02),
        'ssm_a_log': jnp.log(jax.random.uniform(ks[8], (DEPTH, SSM_HEADS), jnp.float32, 1.0, 16.0)),
        'ssm_dt_bias': dt0 + jnp.log(-jnp.expm1(-dt0)),
        'ssm_d': 1.0 + nrm(ks[10], (DEPTH, SSM_HEADS), 0.02),
        'ssm_conv_w': nrm(ks[11], (DEPTH, SSM_CONV, SSM_CONV_CH), SSM_CONV ** -0.5),
        'ssm_conv_b': nrm(ks[12], (DEPTH, SSM_CONV_CH), 0.02),
        'ssm_norm_w': 1.0 + nrm(ks[13], (DEPTH, SSM_WIDTH), 0.02),
        'w_out': nrm(ks[14], (DEPTH, D_MIX, D_MODEL), D_MIX ** -0.5),
        'norm2_w': 1.0 + nrm(ks[15], (DEPTH, D_MODEL), 0.02),
        'router_w': nrm(ks[16], (DEPTH, D_MODEL, N_EXPERTS), D_MODEL ** -0.5),
        'router_b': nrm(ks[17], (DEPTH, N_EXPERTS), 0.01),
        'exp_w1': nrm(ks[18], (DEPTH, N_EXPERTS, D_MODEL, 2 * D_FF), D_MODEL ** -0.5),
        'exp_b1': nrm(ks[19], (DEPTH, N_EXPERTS, 2 * D_FF), 0.01),
        'exp_w2': nrm(ks[20], (DEPTH, N_EXPERTS, D_FF, D_MODEL), D_FF ** -0.5),
        'exp_b2': nrm(ks[21], (DEPTH, N_EXPERTS, D_MODEL), 0.01),
        'final_norm_w': 1.0 + nrm(ks[22], (D_MODEL,), 0.02),
    }

def reference(x, c, ada_w, ada_b, norm1_w, w_in, hg_lb_logits, hg_norm_w, ssm_a_log, ssm_dt_bias,
              ssm_d, ssm_conv_w, ssm_conv_b, ssm_norm_w, w_out, norm2_w, router_w, router_b,
              exp_w1, exp_b1, exp_w2, exp_b2, final_norm_w):
    lb_all = jnp.cumsum(jax.nn.softmax(hg_lb_logits.astype(jnp.float32), axis=0), axis=0)
    c_act = jax.nn.silu(c)
    for l in range(DEPTH):
        mod = c_act @ ada_w[l] + ada_b[l]
        sh1, sc1, g1, sh2, sc2, g2 = jnp.split(mod, N_MOD, axis=-1)
        h = modulate(rmsnorm(x, norm1_w[l]), sh1, sc1)
        x = x + g1[:, None, :] * hybrid_mixer(h, w_in[l], lb_all[l], hg_norm_w[l], ssm_a_log[l],
                                              ssm_dt_bias[l], ssm_d[l], ssm_conv_w[l], ssm_conv_b[l],
                                              ssm_norm_w[l], w_out[l])
        h = modulate(rmsnorm(x, norm2_w[l]), sh2, sc2)
        x = x + g2[:, None, :] * moe_ffn(h, router_w[l], router_b[l], exp_w1[l], exp_b1[l],
                                         exp_w2[l], exp_b2[l])
    return rmsnorm(x, final_norm_w)


_drawn_inputs = setup_inputs


def setup_inputs(seed=0):
    import zlib

    import numpy as np

    out = dict(_drawn_inputs(seed))
    spreads = {}
    factors = {'norm1_w': 6.148,
     'hg_lb_logits': 8.0,
     'hg_norm_w': 7.502,
     'ssm_d': 200.0,
     'ssm_conv_b': 43.616,
     'ssm_norm_w': 48.84,
     'norm2_w': 14.767,
     'router_b': 34.129,
     'exp_b1': 57.727,
     'exp_b2': 200.0,
     'final_norm_w': 22.588}
    for name, (base, spread) in spreads.items():
        noise = np.random.default_rng([zlib.crc32(name.encode()), seed]).standard_normal(out[name].shape)
        drawn = base * np.exp(spread * noise) if base else spread * noise
        out[name] = jnp.asarray(drawn.astype(out[name].dtype))
    for name, factor in factors.items():
        out[name] = (out[name] * factor).astype(out[name].dtype)
    return out
```

```python
from contextlib import ExitStack

import concourse.bass as bass
from concourse import mybir

F32 = mybir.dt.float32
BF16 = mybir.dt.bfloat16
I32 = mybir.dt.int32
U32 = mybir.dt.uint32
ALU = mybir.AluOpType
ACT = mybir.ActivationFunctionType
AX_X = mybir.AxisListType.X

P = 128
D = 1024
KD = D // P
TOK = 512
TT = TOK // P
EPS = 1e-6
HEADS = 4
HG = 512
CHUNK = 64
CHUNKS = TOK // CHUNK
SSM_HEADS = 8
CONV = 4
EXPERTS = 32
TOP = 4
FF = 1024
LIMIT = 7.0
ALPHA = 1.702
HALF = 512
EXTRA = 16
BLOCKS = EXPERTS + EXTRA
MAX_BLOCKS = EXPERTS + (TOK * TOP - EXPERTS) // P
SLOT_GROUPS = TOK // P
UNUSED = TOK

C_ADAB, C_N1, C_N2, C_CW, C_CB, C_LB, C_HGN, C_SSMN, C_C = 0, 48, 56, 64, 96, 104, 112, 113, 117
SMALL_ROWS = 125

QUARTERS = [(j, CHUNK * (j // 2) + 32 * (j % 2), CHUNK * (j // 2) + CHUNK) for j in range(4)]

Q_COL, F_COL, I_COL, G_COL, Z_COL, X_COL, DT_COL = 0, 512, 1024, 1536, 2048, 2560, 3584
LOADS = ([("ada", j) for j in range(4)]
         + [("in", c) for c in (Q_COL, F_COL, I_COL, G_COL, X_COL, X_COL + HALF, Z_COL)]
         + [("ada", j) for j in range(4, 12)] + [("out", 0), ("out", 1)])
L_IN, L_ADA2, L_OUT = 4, 11, 19

UNITS = ([("q", i, L_IN, "dve") for i in range(4)] + [("f", i, L_IN + 1, "act") for i in range(4)]
         + [("i", i, L_IN + 2, "act") for i in range(4)] + [("g", i, L_IN + 3, "dve") for i in range(4)]
         + [("x", i, L_IN + 4 + i // 4, "dve") for i in range(8)] + [("dt", 0, None, "dve")]
         + [("z", i, L_IN + 6, "dve") for i in range(4)])


def evacuated(u):
    who = UNITS[u][3]
    return who, sum(x[3] == who for x in UNITS[:u + 1])


GATED = [u for u, x in enumerate(UNITS) if x[0] in ("q", "g", "z", "x")]


def gated_done(n):
    return evacuated(GATED[n])[1]


def build(nc, x, c, ada_w, ada_b, norm1_w, w_in, hg_lb_logits, hg_norm_w, ssm_a_log, ssm_dt_bias,
          ssm_d, ssm_conv_w, ssm_conv_b, ssm_norm_w, w_out, norm2_w, router_w, router_b,
          exp_w1, exp_b1, exp_w2, exp_b2, final_norm_w, out):
    with ExitStack() as ctx:
        def sb(name, shape, dt=F32):
            return ctx.enter_context(nc.sbuf_tensor(name, shape, dt))

        def sem(name):
            return ctx.enter_context(nc.semaphore(name))

        psum = ctx.enter_context(nc.psum_tensor("banks", [P, 8 * HALF], F32))

        def bank(b, n=1):
            return psum[:, b * HALF:(b + n) * HALF]

        xhat_dram = nc.dram_tensor("xhat_rows", [TOK, D], F32, kind="Internal").ap()
        moe_dram = nc.dram_tensor("moe_rows", [TOK, D], F32, kind="Internal").ap()

        w1_ring = sb("w1_ring", [P, KD, 2 * FF])
        w2_ring = sb("w2_ring", [P, KD, D])
        x_sb = sb("x_sb", [P, TT, D])
        g1_b = sb("g1_b", [P, D])
        g2_b = sb("g2_b", [P, D])
        ht = sb("ht", [P, KD, TOK])
        xc = sb("xc", [P, KD * TOK])
        qb, fb, kb, vb, gb, zb = (sb(n, [P, 2048]) for n in ("qb", "fb", "kb", "vb", "gb", "zb"))
        ident = sb("ident", [P, P])
        tri = sb("tri", [P, P])
        ones = sb("ones", [P, P])
        block_mask = sb("block_mask", [P, P])
        cols = sb("cols", [P, P])
        row = sb("row", [P, HALF])
        rw = sb("rw", [P, KD, EXPERTS])
        misc = sb("misc", [P, 560])

        at = [0]

        def small(n, parts=P):
            a = at[0]
            at[0] += n
            assert at[0] <= 560
            return misc[0:parts, a:a + n]

        win = w2_ring[:, :, :].rearrange("p k n -> p (k n)").rearrange("p (b k n) -> p b k n", b=2, k=KD)
        w1_flat = w1_ring[:, :, :].rearrange("p k n -> p (k n)")
        ks = w1_flat[:, 0:2048]
        qep = w1_flat[:, 2048:6144].rearrange("p (h c s) -> p h c s", h=HEADS, c=CHUNKS)
        vp = w1_flat[:, 6144:10240].rearrange("p (c n) -> p c n", c=CHUNKS)
        sr = w1_flat[:, 10240:12288]
        klt = w1_flat[:, 12288:14336]
        sig_tmp = w1_flat[:, 14336:15360].rearrange("p (b n) -> p b n", b=2)
        conv_tmp = w1_flat[:, 15360:16384].rearrange("p (b n) -> p b n", b=2)
        small_rows = ks[0:SMALL_ROWS, 0:P]
        scan_mask = zb

        xh = xc[:, :].rearrange("p (t d) -> p t d", t=TT)
        xbc = xc[:, :].rearrange("p (k t) -> p k t", k=KD)

        def by_head(a):
            return a.rearrange("p (h t) -> p h t", h=HEADS)

        def by_tile(a):
            return a.rearrange("p (t n) -> p t n", t=TT)

        q3, f3, k3, ks3 = by_head(qb[:, :]), by_head(fb[:, :]), by_head(kb[:, :]), by_head(ks)
        v3, g3, z3, att3, klt3, sr3 = (by_tile(a) for a in (vb[:, :], gb[:, :], zb[:, :], fb[:, :], klt, sr))

        mod = small(48)
        s1c, s2c, c_act, c_sig = small(8), small(8), small(8), small(8)
        lb0, lb1, lbs, oml = small(4), small(4), small(4), small(4)
        ssq, rstd = small(4), small(4)
        dec = small(32)
        ssh, rh = small(16), small(16)
        dtb, alog, skip = small(8), small(8), small(8)
        dtr, dtv, dta, dt_tmp, acum, ea = (small(32) for _ in range(6))
        na = small(8)
        last, wgt, eal = small(8), small(8), small(8)
        wdt = small(64).rearrange("p (k n) -> p k n", k=KD)
        rb = small(32)
        eps = small(1)

        S = {n: sem(n) for n in (
            "pool_order", "dve_order", "act_order", "consts_ready", "pads_ready", "small_landed", "x_landed",
            "bias_landed", "gate_bias_landed", "dt_w_landed", "cols_turned", "cols_ready", "c_sig_ready",
            "c_ready", "row_done", "row_copied", "spread_done", "mod_done", "sq_ready", "root_ready", "xh_ready",
            "xt_done", "ht_ready", "win_used", "proj_done", "evac_act", "evac_dve", "sig_ready",
            "conv_ready", "hg_dve", "hg_act", "lb_act", "att_done", "att_masked", "klt_turned",
            "klt_ready", "vp_ready", "ds_done", "s_ready", "o_done", "o_sq", "o_normed",
            "dt_dve", "dt_act", "acum_done", "acum_ready", "ea_ready", "m_turned", "dtri_ready", "acb_done",
            "m_copied", "m_seg", "m_exp", "m_ready", "my_done", "m_free", "m_gated", "m_sq", "y_ready",
            "mt_turned", "mt_ready", "mix_done", "x2_ready", "sq2_ready", "xh2_ready", "xh2_stored",
            "xt2_done", "ht2_ready", "rw_landed", "logits_done", "b1_landed", "b1_ready", "b2_landed",
            "iota_ready", "route", "route_pe", "route_act", "tables_ready", "moe_init", "moe_stored",
            "xg_zero", "stage", "dma_go", "xg_landed", "tx_done", "xgt_ready", "sel_ready", "h_done", "w1_used",
            "w2_used", "clipped", "lin_ready", "sig2_ready", "act_ready", "ta_done", "actt_ready",
            "y_done", "ys_ready", "scattered", "moe_landed", "fin", "fin_act", "fnw_landed", "out_ready", "out_stored")}
        win_landed = [sem(f"win_landed{i}") for i in range(2)]
        w1_landed = [sem(f"w1_landed{i}") for i in range(KD)]
        w2_landed = [sem(f"w2_landed{i}") for i in range(KD)]

        xs, xdt, xw, yt = (qb[:, i * 512:(i + 1) * 512] for i in range(4))
        seg = kb[:, 0:1024].rearrange("p (h t) -> p h t", h=SSM_HEADS)
        dtri = kb[:, 1024:2048].rearrange("p (h t) -> p h t", h=SSM_HEADS)
        btk = vb[:, 0:256]
        cbm = vb[:, 256:512].rearrange("p (g t) -> p g t", g=2)
        sm = vb[:, 512:1024]
        m_tmp = vb[:, 1024:1536]
        m_junk = vb[:, 1536:2048]

        o = [0]

        def cut(n):
            a = o[0]
            o[0] += n
            assert o[0] <= 4096
            return xc[:, a:a + n]

        onehot, onehot_p = cut(512), cut(512)
        member = cut(128).rearrange("p (t e) -> p t e", t=TT)
        member3 = cut(384).rearrange("p (t r e) -> p t r e", t=TT, r=3)
        lo_hot = cut(256).rearrange("p (b s) -> p b s", b=2)
        key_hot = cut(512).rearrange("p (b n) -> p b n", b=2)
        b2_sb = cut(1024)[0:EXPERTS, :]
        gates_t = cut(512)[0:EXPERTS, :]
        logits = cut(128).rearrange("p (t e) -> p t e", t=TT)
        gate_dense = cut(128).rearrange("p (t e) -> p t e", t=TT)
        o2 = [0]

        def cut2(n, dt=None):
            a = o2[0]
            o2[0] += n
            assert o2[0] <= 2048
            v = qb[:, a:a + n]
            return v.bitcast(dt) if dt is not None else v

        top8, idx8f = cut2(32), cut2(32)
        idx8 = cut2(32, U32)
        gate_e, gate_s, gate_r, gates = cut2(16), cut2(4), cut2(4), cut2(16)
        pos, pos_k, hi1, hi2, hi, lo, key = cut2(128), cut2(16), cut2(16), cut2(16), cut2(16), cut2(16), cut2(16)
        more, more_pos, ext_hot, ext_sel = cut2(1), cut2(1), cut2(16), cut2(128)
        iota = cut2(128)
        tris = cut2(128)
        tok_id, thr, col_q, mod32 = cut2(16), cut2(1), cut2(1), cut2(1)
        col_bc, mod_bc = cut2(128), cut2(128)
        tab_f = cut2(2 * BLOCKS).rearrange("p (a b) -> p a b", a=2)
        slot_tok = row[:, 0:P].bitcast(I32)
        slot_gate = row[:, P:2 * P]
        blk_hot = row[:, 256:256 + BLOCKS]
        tab = row[0:1, 304:304 + 2 * BLOCKS + 1].bitcast(I32)
        tab_e, tab_col, tab_n = tab[:, 0:BLOCKS], tab[:, BLOCKS:2 * BLOCKS], tab[:, 2 * BLOCKS:2 * BLOCKS + 1]
        stage_g = row[:, 408:409].bitcast(I32)
        stage_s = row[:, 409:410].bitcast(I32)

        xg, xgt = vb[:, 0:1024], vb[:, 1024:2048].rearrange("p (k s) -> p k s", k=KD)
        glu, lin = kb[:, 0:1024], kb[:, 1024:2048]
        act_sb = fb[:, 0:1024]
        actt = fb[:, 1024:2048].rearrange("p (k s) -> p k s", k=KD)
        ys, sg = gb[:, 0:1024], gb[:, 1024:2048]
        sel = ones[:, 0:64].bitcast(BF16)
        b1_raw = ht[:, 0:4, :].rearrange("p k t -> p (k t)")
        b1_parts = zb[:, 0:1024].bitcast(BF16)
        fnw = zb[:, 1024:2048]

        def order(name):
            n = [0]

            def step(ins):
                n[0] += 1
                ins.then_inc(S[name], 1)

            def settle(eng):
                eng.wait_ge(S[name], n[0])

            return step, settle

        block = ctx.enter_context(nc.Block())

        def at_least(eng, s, value):
            if not isinstance(value, int) or value > 0:
                eng.wait_ge(s, value)

        @block.sync
        def _(sp):
            rows = lambda a, n: a.rearrange("a (k p) -> (a k) p", p=P)
            r0 = 0
            for src in (rows(ada_b, 48), rows(norm1_w, 8), rows(norm2_w, 8),
                        ssm_conv_w[0].rearrange("j (k p) -> (j k) p", p=P), rows(ssm_conv_b, 8),
                        hg_lb_logits.rearrange("l (k p) -> (l k) p", p=P), hg_norm_w, rows(ssm_norm_w, 4),
                        rows(c, 8)):
                n = src.shape[0]
                sp.dma_start(small_rows[r0:r0 + n, :], src).then_inc(S["small_landed"], 16)
                r0 += n
            assert r0 == SMALL_ROWS
            xv = x[0].rearrange("(t p) d -> p t d", p=P)
            sp.dma_start(x_sb[:, :, :], xv).then_inc(S["x_landed"], 16)
            ada_v = ada_w[0].rearrange("(k p) n -> p k n", p=P)
            in_v = w_in[0].rearrange("(k p) n -> p k n", p=P)
            out_v = w_out[0].rearrange("(k p) n -> p k n", p=P)
            for n, (kind, j) in enumerate(LOADS):
                if n >= 2:
                    sp.wait_ge(S["win_used"], n - 1)
                src = ada_v if kind == "ada" else in_v if kind == "in" else out_v
                a = j if kind == "in" else j * HALF
                sp.dma_start(win[:, n % 2], src[:, :, a:a + HALF]).then_inc(win_landed[n % 2], 16)
                if n == 4:
                    for dst, src in ((dtb, ssm_dt_bias), (alog, ssm_a_log), (skip, ssm_d), (rb, router_b)):
                        sp.dma_start(dst, src[0].partition_broadcast(P)).then_inc(S["bias_landed"], 16)
                    sp.dma_start(wdt, in_v[:, :, DT_COL:DT_COL + 8]).then_inc(S["dt_w_landed"], 16)
                    for dst, a in ((g1_b, 2 * D), (g2_b, 5 * D)):
                        sp.dma_start(dst[:, :], ada_b[0, a:a + D].partition_broadcast(P)).then_inc(
                            S["gate_bias_landed"], 16)
                    sp.dma_start(rw[:, :, :], router_w[0].rearrange("(k p) n -> p k n", p=P)).then_inc(
                        S["rw_landed"], 16)

            def load_w1(e, b):
                for k in range(KD):
                    at_least(sp, S["w1_used"], b * KD - KD + k + 1)
                    sp.dma_start(w1_ring[:, k, :], exp_w1[0, e, k * P:(k + 1) * P, :]).then_inc(w1_landed[k], 16)

            def load_w2(e, b):
                for k in range(KD):
                    at_least(sp, S["w2_used"], b * KD - KD + k + 1)
                    sp.dma_start(w2_ring[:, k, :], exp_w2[0, e, k * P:(k + 1) * P, :]).then_inc(w2_landed[k], 16)

            sp.wait_ge(S["o_normed"], TT)
            load_w1(0, 0)
            for t in range(TT):
                sp.wait_ge(S["xh2_ready"], t + 1)
                sp.dma_start(xhat_dram[t * P:(t + 1) * P, :], xh[:, t]).then_inc(S["xh2_stored"], 16)
            sp.wait_ge(S["xh2_stored"], 16 * TT)
            sp.wait_ge(S["xt2_done"], KD)
            sp.dma_start(b2_sb, exp_b2[0]).then_inc(S["b2_landed"], 16)
            sp.wait_ge(S["logits_done"], 1)
            for i in range(3):
                sp.dma_start(b1_raw[32 * i:32 * i + 32, :], exp_b1[0]).then_inc(S["b1_landed"], 16)
            sp.dma_start(fnw, final_norm_w.partition_broadcast(P)).then_inc(S["fnw_landed"], 16)
            sp.wait_ge(S["tables_ready"], 1)
            n_more = sp.value_load(tab_n, min_val=EXPERTS - 2, max_val=MAX_BLOCKS - 2)
            load_w1(1, 1)
            sp.wait_ge(S["win_used"], len(LOADS))
            load_w2(0, 0)
            with sp.Fori(0, n_more) as i:
                b = i + 2
                e = sp.value_load(tab_e[:, bass.ds(b, 1)], min_val=0, max_val=EXPERTS - 1)
                e_before = sp.value_load(tab_e[:, bass.ds(b - 1, 1)], min_val=0, max_val=EXPERTS - 1)
                load_w1(e, b)
                load_w2(e_before, b - 1)
            e_last = sp.value_load(tab_e[:, bass.ds(n_more + 1, 1)], min_val=0, max_val=EXPERTS - 1)
            load_w2(e_last, n_more + 1)
            sp.wait_ge(S["scattered"], n_more * 16 + 32)
            for t in range(TT):
                sp.dma_start(xh[:, t], moe_dram[t * P:(t + 1) * P, :]).then_inc(S["moe_landed"], 16)
                sp.wait_ge(S["moe_landed"], 16 * (t + 1))
            for t in range(TT):
                sp.wait_ge(S["out_ready"], t + 1)
                sp.dma_start(out[0, t * P:(t + 1) * P, :], x_sb[:, t]).then_inc(S["out_stored"], 16)
            sp.wait_ge(S["out_stored"], 16 * TT)

        @block.gpsimd
        def _(pool):
            step, settle = order("pool_order")
            step(pool.memset(ident[:, :], 0.0))
            step(pool.memset(eps, EPS))
            step(pool.memset(tri[:, :], 1.0))
            step(pool.memset(block_mask[:, :], 1.0))
            step(pool.memset(ones[:, :], 1.0))
            step(pool.memset(scan_mask[:, :], 1.0))
            settle(pool)
            step(pool.affine_select(out=ident[:, :], in_=ident[:, :], compare_op=ALU.not_equal, fill=1.0, base=0,
                                    pattern=[[-1, P]], channel_multiplier=1))
            for m in (tri, block_mask):
                step(pool.affine_select(out=m[:, :], in_=m[:, :], compare_op=ALU.is_ge, fill=0.0, base=0,
                                        pattern=[[1, P]], channel_multiplier=-1))
            step(pool.memset(scan_mask[:, :].rearrange("p (c s) -> p c s", s=CHUNK)[:, :, 0:1], 0.0))
            settle(pool)
            pool.memset(block_mask[0:64, 64:128], 0.0).then_inc(S["consts_ready"], 1)
            step(pool.memset(qep, 0.0))
            settle(pool)
            pool.memset(vp, 0.0).then_inc(S["pads_ready"], 1)
            pool.wait_ge(S["pads_ready"], 1)
            pool.wait_ge(S["evac_act"], 8)
            vp4 = vp.rearrange("p (t a) n -> p t a n", a=2)
            pool.tensor_copy(vp4[0:64, :, 0, :], v3[0:64]).then_inc(S["vp_ready"], 1)
            pool.tensor_copy(vp4[64:128, :, 1, :], v3[64:128]).then_inc(S["vp_ready"], 1)

            pool.wait_ge(S["y_ready"], TT)
            step(pool.iota(iota, pattern=[[1, P]], base=0, channel_multiplier=0, allow_small_or_imprecise_dtypes=True))
            step(pool.memset(tris, 1.0))
            step(pool.iota(tok_id, pattern=[[P, TT], [0, TOP]], base=-UNUSED, channel_multiplier=1,
                           allow_small_or_imprecise_dtypes=True))
            step(pool.iota(col_q, pattern=[[0, 1]], base=EXPERTS, channel_multiplier=1,
                           allow_small_or_imprecise_dtypes=True))
            step(pool.iota(col_bc, pattern=[[0, P]], base=EXPERTS, channel_multiplier=1,
                           allow_small_or_imprecise_dtypes=True))
            for q in range(4):
                rows = slice(32 * q, 32 * q + 32)
                settle(pool)
                step(pool.memset(thr[rows, :], float(P * (q + 1))))
                settle(pool)
                step(pool.iota(mod32[rows, :], pattern=[[0, 1]], base=0, channel_multiplier=1,
                               allow_small_or_imprecise_dtypes=True))
                settle(pool)
                step(pool.iota(mod_bc[rows, :], pattern=[[0, P]], base=0, channel_multiplier=1,
                               allow_small_or_imprecise_dtypes=True))
            settle(pool)
            step(pool.iota(tab_f, pattern=[[0, 2], [1, BLOCKS]], base=0, channel_multiplier=0,
                           allow_small_or_imprecise_dtypes=True))
            settle(pool)
            pool.affine_select(out=tris, in_=tris, compare_op=ALU.is_ge, fill=0.0, base=-1, pattern=[[1, P]],
                               channel_multiplier=-1).then_inc(S["iota_ready"], 1)
            pool.wait_ge(S["b1_landed"], 48)
            pool.wait_ge(S["mt_turned"], KD)
            step(pool.tensor_copy(b1_parts[0:96, :], b1_raw[0:96, :]))
            settle(pool)
            for first in (32, 64):
                for r in range(first, 96, 32):
                    step(pool.tensor_tensor(b1_raw[r:r + 32, :], b1_raw[r:r + 32, :], b1_parts[r:r + 32, :],
                                            ALU.subtract))
                    settle(pool)
                for r in range(first, 96, 32):
                    step(pool.tensor_copy(b1_parts[r:r + 32, :], b1_raw[r:r + 32, :]))
                    settle(pool)
            pool.memset(xg, 0.0).then_inc(S["b1_ready"], 1)
            pool.wait_ge(S["b1_ready"], 1)
            pool.wait_ge(S["xh2_stored"], 16 * TT)

            pool.wait_ge(S["tables_ready"], 1)
            n_more = pool.value_load(tab_n, min_val=EXPERTS - 2, max_val=MAX_BLOCKS - 2)

            def column(b):
                return pool.value_load(tab_col[:, bass.ds(b, 1) if not isinstance(b, int) else slice(b, b + 1)],
                                       min_val=0, max_val=P - 1)

            def gather(b, staged):
                col, limit = column(b), pool.to_reg(TOK - 1)
                at_least(pool, S["tx_done"], b)
                pool.tensor_copy(stage_g, slot_tok[:, bass.ds(col, 1)]).then_inc(S["stage"], 1)
                pool.wait_ge(S["stage"], staged)
                pool.sem_inc(S["dma_go"], 1)
                pool.indirect_dma_start(xg, None, xhat_dram, bass.IndirectOffsetOnAxis(stage_g, 0),
                                        bounds_check=limit, oob_is_err=False).then_inc(S["xg_landed"], 16)

            def scatter(b, staged):
                col, limit = column(b), pool.to_reg(TOK - 1)
                at_least(pool, S["scattered"], b * 16)
                pool.tensor_copy(stage_s, slot_tok[:, bass.ds(col, 1)]).then_inc(S["stage"], 1)
                pool.wait_ge(S["stage"], staged)
                pool.wait_ge(S["ys_ready"], b + 1)
                pool.sem_inc(S["dma_go"], 1)
                pool.indirect_dma_start(moe_dram, bass.IndirectOffsetOnAxis(stage_s, 0), ys, None,
                                        bounds_check=limit, oob_is_err=False,
                                        compute_op=ALU.add).then_inc(S["scattered"], 16)

            gather(0, 1)
            gather(1, 2)
            pool.wait_ge(S["moe_stored"], 16 * 2 * TT)
            with pool.Fori(0, n_more) as i:
                b = i + 2
                gather(b, 2 * b - 1)
                scatter(b - 2, 2 * b)
            scatter(n_more, 2 * n_more + 3)
            scatter(n_more + 1, 2 * n_more + 4)

        @block.scalar
        def _(act):
            act.wait_ge(S["cols_ready"], 1)
            act.activation(c_sig, cols[:, C_C:C_C + 8], ACT.Sigmoid).then_inc(S["c_sig_ready"], 1)

            def root(sums, n, done, value):
                act.wait_ge(S[done], value)
                act.activation(sums, sums, ACT.Sqrt, bias=eps, scale=1.0 / n).then_inc(S["root_ready"], 1)

            act.wait_ge(S["x_landed"], 16)
            for t in range(TT):
                act.activation(xh[:, t], x_sb[:, t], ACT.Square, accum_out=ssq[:, t:t + 1]).then_inc(S["sq_ready"], 1)
            root(ssq, D, "sq_ready", TT)

            def row_copy(j):
                act.wait_ge(S["row_done"], j + 1)
                at_least(act, S["spread_done"], j)
                src = bank(j % 2 if j < 4 else 7)
                act.activation(row[0:1, :], src[0:1, :], ACT.Copy).then_inc(S["row_copied"], 1)

            for j in range(4):
                row_copy(j)
            act.wait_ge(S["lb_act"], 2)
            act.activation(lb0, lb0, ACT.Exp).then_inc(S["lb_act"], 1)
            act.activation(lb1, lb1, ACT.Exp).then_inc(S["lb_act"], 1)
            act.wait_ge(S["mod_done"], 5)
            for k in range(KD):
                act.wait_ge(S["xt_done"], k + 1)
                act.activation(ht[:, k, :], bank(2 + k % 4), ACT.Identity, bias=mod[:, k:k + 1],
                               scale=s1c[:, k:k + 1]).then_inc(S["ht_ready"], 1)

            def hg(i):
                if i == 1:
                    act.wait_ge(S["hg_dve"], 5)
                    act.activation(ks, fb[:, :], ACT.Ln).then_inc(S["hg_act"], 1)
                elif i == 3:
                    act.wait_ge(S["hg_dve"], 7)
                    act.activation(sr, fb[:, :], ACT.Exp).then_inc(S["hg_act"], 1)
                    act.activation(ks, klt, ACT.Exp).then_inc(S["hg_act"], 1)
                elif i == 5:
                    act.wait_ge(S["hg_dve"], 10)
                    act.activation(ks, klt, ACT.Exp, scale=-1.0).then_inc(S["hg_act"], 1)
                elif i == 7:
                    act.wait_ge(S["hg_dve"], 12)
                    act.activation(sr, klt, ACT.Exp).then_inc(S["hg_act"], 1)
                    act.activation(dec.rearrange("p (h c) -> p h c", h=HEADS),
                                   f3.rearrange("p h (c s) -> p h c s", s=CHUNK)[:, :, :, CHUNK - 1],
                                   ACT.Exp).then_inc(S["hg_act"], 1)

            for u, (kind, i, _, _) in enumerate(UNITS):
                src = bank(u % 3)
                if u in GATED:
                    n = GATED.index(u)
                    if kind == "x":
                        act.wait_ge(S["conv_ready"], i + 1)
                        src = conv_tmp[:, i % 2]
                    else:
                        act.wait_ge(S["proj_done"], u + 1)
                    if n >= 2:
                        act.wait_ge(S["evac_dve"], gated_done(n - 2))
                    act.activation(sig_tmp[:, n % 2], src, ACT.Sigmoid).then_inc(S["sig_ready"], 1)
                elif kind == "f":
                    act.wait_ge(S["proj_done"], u + 1)
                    act.activation(f3[:, i], src, ACT.Sigmoid).then_inc(S["evac_act"], 1)
                elif kind == "i":
                    act.wait_ge(S["proj_done"], u + 1)
                    act.activation(v3[:, i], src, ACT.Copy).then_inc(S["evac_act"], 1)
                if 7 <= u <= 15:
                    hg(u - 7)
            for t in range(TT):
                act.wait_ge(S["klt_turned"], t + 1)
                act.activation(klt3[:, t], bank(t % 3), ACT.Copy).then_inc(S["klt_ready"], 1)

            def o_square(t):
                act.wait_ge(S["o_done"], t + 1)
                for h in range(HEADS):
                    act.activation(sig_tmp[:, 0, h * P:(h + 1) * P], bank(t % 3)[:, h * P:(h + 1) * P], ACT.Square,
                                   accum_out=ssh[:, 4 * t + h:4 * t + h + 1]).then_inc(S["o_sq"], 1)
                root(ssh[:, 4 * t:4 * t + 4], P, "o_sq", 4 * t + 4)

            row_copy(4)
            o_square(0)
            row_copy(5)
            o_square(1)
            row_copy(6)
            o_square(2)
            o_square(3)
            row_copy(7)

            act.wait_ge(S["dt_dve"], 1)
            act.activation(dt_tmp, dt_tmp, ACT.Exp, scale=-1.0).then_inc(S["dt_act"], 1)
            act.activation(na, alog, ACT.Exp).then_inc(S["dt_act"], 1)
            act.wait_ge(S["dt_act"], 1)
            act.activation(dt_tmp, dt_tmp, ACT.Ln, bias=1.0).then_inc(S["dt_act"], 1)
            act.wait_ge(S["acum_ready"], 1)
            act.activation(ea, acum, ACT.Exp).then_inc(S["ea_ready"], 1)
            for t in range(TT):
                act.wait_ge(S["m_turned"], t + 1)
                act.activation(xs, bank(0), ACT.Copy).then_inc(S["m_copied"], 1)
                act.activation(btk, bank(1)[:, 0:256], ACT.Copy).then_inc(S["m_copied"], 1)
                act.wait_ge(S["m_seg"], t + 1)
                act.activation(seg, seg, ACT.Exp).then_inc(S["m_exp"], 1)
                act.activation(wgt, wgt, ACT.Exp).then_inc(S["m_exp"], 1)
                act.activation(eal, last, ACT.Exp).then_inc(S["m_exp"], 1)
                row_copy(8 + t)
                act.wait_ge(S["m_gated"], t + 1)
                for g in range(2):
                    act.activation(m_junk[:, g * 256:(g + 1) * 256], z3[:, t, g * 256:(g + 1) * 256], ACT.Square,
                                   accum_out=ssh[:, 2 * t + g:2 * t + g + 1]).then_inc(S["m_sq"], 1)
                root(ssh[:, 2 * t:2 * t + 2], 256, "m_sq", 2 * t + 2)
            for k in range(KD):
                act.wait_ge(S["mt_turned"], k + 1)
                w = cols[:, C_HGN:C_HGN + 1] if k < 4 else cols[:, C_SSMN + k - 4:C_SSMN + k - 3]
                act.activation(ht[:, k, :], bank(k % 4), ACT.Copy, scale=w).then_inc(S["mt_ready"], 1)
            for t in range(TT):
                act.wait_ge(S["x2_ready"], 5 + t)
                act.activation(xh[:, t], x_sb[:, t], ACT.Square, accum_out=ssq[:, t:t + 1]).then_inc(S["sq2_ready"], 1)
            root(ssq, D, "sq2_ready", TT)
            for k in range(KD):
                act.wait_ge(S["xt2_done"], k + 1)
                act.activation(ht[:, k, :], bank(k % 4), ACT.Identity, bias=mod[:, 24 + k:25 + k],
                               scale=s2c[:, k:k + 1]).then_inc(S["ht2_ready"], 1)
            act.wait_ge(S["route_act"], 1)
            act.activation(gate_e, gate_e, ACT.Exp).then_inc(S["route_act"], 1)
            for n in range(2 * TT):
                act.wait_ge(S["moe_init"], n + 1)
                if n == 4:
                    act.wait_ge(S["moe_stored"], 16 * 4)
                act.activation(ht[:, 4 + n % 4, :], bank(4 + n % 2), ACT.Copy).then_inc(S["fin_act"], 1)
                act.wait_ge(S["fin_act"], n + 1)
                t, h = n // 2, n % 2
                act.dma_start(moe_dram[t * P:(t + 1) * P, h * HALF:(h + 1) * HALF], ht[:, 4 + n % 4, :]).then_inc(
                    S["moe_stored"], 16)

            act.wait_ge(S["tables_ready"], 1)
            n_more = act.value_load(tab_n, min_val=EXPERTS - 2, max_val=MAX_BLOCKS - 2)

            def sigmoid(b):
                act.wait_ge(S["clipped"], 2 * b + 1)
                act.activation(sg, glu, ACT.Sigmoid, scale=ALPHA).then_inc(S["sig2_ready"], 1)

            def results(b):
                col = act.value_load(tab_col[:, bass.ds(b, 1)], min_val=0, max_val=P - 1)
                act.wait_ge(S["y_done"], b + 1)
                at_least(act, S["scattered"], b * 16)
                act.activation(ys, bank(4, 2), ACT.Copy, scale=slot_gate[:, bass.ds(col, 1)]).then_inc(S["ys_ready"], 1)

            def turned(b):
                act.wait_ge(S["ta_done"], b + 1)
                act.activation(actt, bank(6, 2), ACT.Copy).then_inc(S["actt_ready"], 1)

            sigmoid(0)
            turned(0)
            with act.Fori(0, n_more) as i:
                b = i + 2
                sigmoid(b - 1)
                results(b - 2)
                turned(b - 1)
            sigmoid(n_more + 1)
            results(n_more)
            turned(n_more + 1)
            results(n_more + 1)
            for t in range(TT):
                act.wait_ge(S["fin"], t + 1)
                act.activation(xh[:, t], x_sb[:, t], ACT.Square, accum_out=ssq[:, t:t + 1]).then_inc(S["fin_act"], 1)
            root(ssq, D, "fin_act", 3 * TT)

        @block.tensor
        def _(pe):
            mm = pe.matmul
            pe.wait_ge(S["small_landed"], 16 * 9)
            pe.wait_ge(S["consts_ready"], 1)
            pe.transpose(bank(6)[:, 0:SMALL_ROWS], small_rows, ident[0:SMALL_ROWS, 0:SMALL_ROWS]).then_inc(
                S["cols_turned"], 1)

            def landed(n):
                pe.wait_ge(win_landed[n % 2], 16 * (n // 2 + 1))

            def ada_row(j):
                n = j if j < 4 else L_ADA2 + j - 4
                b = j % 2 if j < 4 else 7
                if j == 0:
                    pe.wait_ge(S["c_ready"], 1)
                elif 2 <= j < 4:
                    pe.wait_ge(S["row_copied"], j - 1)
                elif j > 4:
                    pe.wait_ge(S["mod_done"], j + 1)
                landed(n)
                for k in range(KD):
                    ins = mm(bank(b)[0:1, :], c_act[:, k:k + 1], win[:, n % 2, k, :], start=(k == 0), stop=(k == KD - 1))
                ins.then_inc(S["row_done"], 1)

            def ada_spread(j):
                pe.wait_ge(S["row_copied"], j + 1)
                dst = bank(2 + j if j < 4 else 7)
                if j in (4, 5, 10, 11):
                    ins = mm(dst, ones[0:1, :], row[0:1, :], start=True, stop=True)
                else:
                    for i in range(4):
                        ins = mm(dst[:, i:i + 1], row[0:1, i * P:(i + 1) * P], ones[0:1, 0:1], start=True, stop=True)
                ins.then_inc(S["spread_done"], 1)

            def release(done, value):
                pe.wait_ge(S[done], value)
                pe.sem_inc(S["win_used"], 1)

            for j in range(4):
                ada_row(j)
                if j >= 1:
                    ada_spread(j - 1)
                release("row_done", j + 1)
            ada_spread(3)
            pe.wait_ge(S["xh_ready"], TT)
            pe.wait_ge(S["mod_done"], 5)
            for k in range(KD):
                if k >= 4:
                    pe.wait_ge(S["ht_ready"], k - 3)
                for t in range(TT):
                    ins = pe.transpose(bank(2 + k % 4)[:, t * P:(t + 1) * P], xh[:, t, k * P:(k + 1) * P], ident[:, :])
                ins.then_inc(S["xt_done"], 1)
            pe.wait_ge(S["ht_ready"], KD)

            for u, (kind, i, n, _) in enumerate(UNITS):
                if u >= 3:
                    who, count = evacuated(u - 3)
                    pe.wait_ge(S["evac_" + who], count)
                b = bank(u % 3)
                if kind == "dt":
                    pe.wait_ge(S["dt_w_landed"], 16)
                    for t in range(TT):
                        for k in range(KD):
                            ins = mm(b[:, 8 * t:8 * t + 8], ht[:, k, t * P:(t + 1) * P], wdt[:, k, :],
                                     start=(k == 0), stop=(k == KD - 1))
                    ins.then_inc(S["proj_done"], 1)
                    continue
                landed(n)
                w = win[:, n % 2]
                j = i % 4
                for k in range(KD):
                    if kind in "qfx":
                        ins = mm(b, w[:, k, j * P:(j + 1) * P], ht[:, k, :], start=(k == 0), stop=(k == KD - 1))
                    else:
                        ins = mm(b, ht[:, k, i * P:(i + 1) * P], w[:, k, :], start=(k == 0), stop=(k == KD - 1))
                ins.then_inc(S["proj_done"], 1)
                if j == 3:
                    release("proj_done", u + 1)

            pe.wait_ge(S["hg_dve"], 14)
            for t in range(TT):
                for h in range(HEADS):
                    for j, a, b in QUARTERS:
                        ins = mm(bank(3 + t)[32 * j:32 * j + 32, h * P + a:h * P + b],
                                 ks3[:, h, t * P + 32 * j:t * P + 32 * j + 32], q3[:, h, t * P + a:t * P + b],
                                 start=True, stop=True, skip_group_check=True)
                ins.then_inc(S["att_done"], 1)
            pe.wait_ge(S["evac_dve"], evacuated(len(UNITS) - 1)[1])
            pe.wait_ge(S["evac_act"], 8)
            for t in range(TT):
                if t == 3:
                    pe.wait_ge(S["klt_ready"], 1)
                for h in range(HEADS):
                    ins = pe.transpose(bank(t % 3)[:, h * P:(h + 1) * P], k3[:, h, t * P:(t + 1) * P], ident[:, :])
                ins.then_inc(S["klt_turned"], 1)

            def ada_filler_row(j):
                ada_row(j)
                release("row_done", j + 1)

            def state(ch):
                if ch == 0:
                    pe.wait_ge(S["att_masked"], 4 * TT)
                    pe.wait_ge(S["vp_ready"], 2)
                if ch >= 4:
                    pe.wait_ge(S["s_ready"], ch - 3)
                pe.wait_ge(S["klt_ready"], ch // 2 + 1)
                for h in range(HEADS):
                    hs = slice(h * P, (h + 1) * P)
                    ins = mm(bank(3 + ch % 4)[:, hs], klt3[:, ch // 2, hs], vp[:, ch, hs], start=True, stop=True)
                ins.then_inc(S["ds_done"], 1)

            def output(t):
                if t == 0:
                    pe.wait_ge(S["klt_ready"], TT)
                if t == 3:
                    pe.wait_ge(S["o_normed"], 1)
                pe.wait_ge(S["s_ready"], 2 * t + 1)
                for h in range(HEADS):
                    hs = slice(h * P, (h + 1) * P)
                    dst = bank(t % 3)[:, hs]
                    mm(dst, att3[:, t, hs], v3[:, t, hs], start=True, stop=False)
                    if t > 0:
                        mm(dst, qep[:, h, 2 * t, :], sr3[:, (2 * t) % 4, hs], start=False, stop=False)
                    ins = mm(dst, qep[:, h, 2 * t + 1, :], sr3[:, (2 * t + 1) % 4, hs], start=False, stop=True)
                ins.then_inc(S["o_done"], 1)

            ada_filler_row(4)
            state(0)
            state(1)
            state(2)
            ada_spread(4)
            output(0)
            state(3)
            state(4)
            ada_filler_row(5)
            ada_spread(5)
            output(1)
            state(5)
            state(6)
            ada_filler_row(6)
            ada_spread(6)
            output(2)
            output(3)
            ada_filler_row(7)
            ada_spread(7)

            pe.wait_ge(S["dt_dve"], 3)
            pe.wait_ge(S["s_ready"], 7)
            mm(bank(6)[:, 0:32], tri[:, :], dta, start=True, stop=True).then_inc(S["acum_done"], 1)
            pe.wait_ge(S["o_normed"], TT)
            for t in range(TT):
                ts = slice(t * P, (t + 1) * P)
                at_least(pe, S["m_free"], t)
                for i in range(4):
                    pe.transpose(bank(0)[:, i * P:(i + 1) * P], xbc[:, i, ts], ident[:, :])
                for g in range(2):
                    pe.transpose(bank(1)[:, g * P:(g + 1) * P], xbc[:, 4 + g, ts], ident[:, :])
                for g in range(2):
                    ins = mm(bank(1)[:, 256 + g * P:256 + (g + 1) * P], xbc[:, 4 + g, ts], xbc[:, 6 + g, ts],
                             start=True, stop=True)
                ins.then_inc(S["m_turned"], 1)
                pe.wait_ge(S["dtri_ready"], t + 1)
                for i in range(2):
                    ins = mm(bank(2 + i), ones[:, :], dtri[:, 4 * i:4 * i + 4, :], start=True, stop=True)
                ins.then_inc(S["acb_done"], 1)
                ada_filler_row(8 + t)
                ada_spread(8 + t)
                pe.wait_ge(S["m_ready"], t + 1)
                for h in range(SSM_HEADS):
                    mm(bank(4)[:, h * 64:(h + 1) * 64], seg[:, h, :], xdt[:, h * 64:(h + 1) * 64], start=True, stop=True)
                if t > 0:
                    for g in range(2):
                        mm(bank(5)[:, g * 256:(g + 1) * 256], xbc[:, 6 + g, ts], sm[:, g * 256:(g + 1) * 256],
                           start=True, stop=True)
                for g in range(2):
                    ins = mm(bank(6)[:, g * 256:(g + 1) * 256], btk[:, g * P:(g + 1) * P],
                             xw[:, g * 256:(g + 1) * 256], start=True, stop=True)
                ins.then_inc(S["my_done"], 1)

            pe.wait_ge(S["y_ready"], TT)
            for k in range(KD):
                if k >= 4:
                    pe.wait_ge(S["mt_ready"], k - 3)
                src = g3 if k < 4 else z3
                for t in range(TT):
                    ins = pe.transpose(bank(k % 4)[:, t * P:(t + 1) * P], src[:, t, (k % 4) * P:(k % 4 + 1) * P],
                                       ident[:, :])
                ins.then_inc(S["mt_turned"], 1)
            pe.wait_ge(S["mt_ready"], KD)
            pe.wait_ge(S["mod_done"], 13)
            for h in range(2):
                landed(L_OUT + h)
                for t in range(TT):
                    u = 4 * h + t
                    at_least(pe, S["x2_ready"], u - 3)
                    for k in range(KD):
                        ins = mm(bank(4 + u % 4), ht[:, k, t * P:(t + 1) * P], win[:, (L_OUT + h) % 2, k, :],
                                 start=(k == 0), stop=(k == KD - 1))
                    ins.then_inc(S["mix_done"], 1)
                release("mix_done", 4 * h + 4)

            pe.wait_ge(S["xh2_ready"], TT)
            for k in range(KD):
                if k >= 4:
                    pe.wait_ge(S["ht2_ready"], k - 3)
                for t in range(TT):
                    ins = pe.transpose(bank(k % 4)[:, t * P:(t + 1) * P], xh[:, t, k * P:(k + 1) * P], ident[:, :])
                ins.then_inc(S["xt2_done"], 1)
            pe.wait_ge(S["ht2_ready"], KD)
            pe.wait_ge(S["rw_landed"], 16)
            for t in range(TT):
                for k in range(KD):
                    ins = mm(bank(4)[:, t * 32:(t + 1) * 32], ht[:, k, t * P:(t + 1) * P], rw[:, k, :],
                             start=(k == 0), stop=(k == KD - 1))
            ins.then_inc(S["logits_done"], 1)

            pe.wait_ge(S["route_pe"], 1)
            pe.wait_ge(S["iota_ready"], 1)
            for t in range(TT):
                for s in range(t):
                    mm(bank(0)[:, t * 32:(t + 1) * 32], ones[:, :], member[:, s, :], start=(s == 0), stop=False)
                ins = mm(bank(0)[:, t * 32:(t + 1) * 32], tris, member[:, t, :], start=(t == 0), stop=True)
            ins.then_inc(S["route"], 1)
            pe.wait_ge(S["route_pe"], 2)
            for t in range(TT):
                ins = mm(bank(1)[0:96, 0:1], member3[:, t, :, :].rearrange("p r e -> p (r e)"), ones[:, 0:1],
                         start=(t == 0), stop=(t == TT - 1))
            ins.then_inc(S["route"], 1)
            pe.wait_ge(S["route_pe"], 3)
            mm(bank(2)[0:96, 0:1], tris[0:96, 0:96], more[0:96, :], start=True, stop=True)
            mm(bank(2)[:, 1:2], ones[0:96, :], more[0:96, :], start=True, stop=True).then_inc(S["route"], 1)
            pe.wait_ge(S["route_pe"], 4)
            mm(bank(3)[:, 0:EXTRA], mod_bc[0:96, :], ext_hot[0:96, :], start=True, stop=True)
            mm(bank(3)[:, EXTRA:2 * EXTRA], col_bc[0:96, :], ext_hot[0:96, :], start=True, stop=True).then_inc(S["route"], 1)
            pe.wait_ge(S["route_pe"], 5)
            for t in range(TT):
                ins = pe.transpose(bank(7)[0:EXPERTS, t * P:(t + 1) * P], gate_dense[:, t, :], ident[:, :])
            ins.then_inc(S["route"], 1)
            for n in range(TT * TOP):
                pe.wait_ge(S["route_pe"], 7 + n)
                ins = mm(bank(4)[:, 0:256], lo_hot[:, n % 2, :], key_hot[:, n % 2, :], start=(n == 0),
                         stop=(n == TT * TOP - 1))
                ins.then_inc(S["route"], 1)
            pe.wait_ge(S["b2_landed"], 16)
            pe.wait_ge(S["tables_ready"], 1)
            for n in range(2 * TT):
                at_least(pe, S["fin_act"], n - 1)
                t, h = n // 2, n % 2
                mm(bank(4 + n % 2), gates_t[:, t * P:(t + 1) * P], b2_sb[:, h * HALF:(h + 1) * HALF],
                   start=True, stop=True).then_inc(S["moe_init"], 1)

            pe.wait_ge(S["b1_ready"], 1)
            n_more = pe.value_load(tab_n, min_val=EXPERTS - 2, max_val=MAX_BLOCKS - 2)

            def turn_x(b):
                pe.wait_ge(S["xg_landed"], 16 * b + 16)
                at_least(pe, S["actt_ready"], b - 1)
                for k in range(KD):
                    ins = pe.transpose(bank(6, 2)[:, k * P:(k + 1) * P], xg[:, k * P:(k + 1) * P], ident[:, :])
                ins.then_inc(S["tx_done"], 1)

            def hidden(b):
                pe.wait_ge(S["xgt_ready"], KD * b + KD)
                pe.wait_ge(S["sel_ready"], b + 1)
                at_least(pe, S["clipped"], 2 * b)
                for n in range(4):
                    mm(bank(n), sel[0:96, :], b1_parts[0:96, n * HALF:(n + 1) * HALF], start=True, stop=False)
                for k in range(KD):
                    pe.wait_ge(w1_landed[k], 16 * b + 16)
                    for n in range(4):
                        ins = mm(bank(n), xgt[:, k, :], w1_ring[:, k, n * HALF:(n + 1) * HALF], start=False,
                                 stop=(k == KD - 1))
                    ins.then_inc(S["w1_used"], 1)

            def turn_act(b):
                pe.wait_ge(S["act_ready"], b + 1)
                at_least(pe, S["xgt_ready"], turned_rows(b))
                for k in range(KD):
                    ins = pe.transpose(bank(6, 2)[:, k * P:(k + 1) * P], act_sb[:, k * P:(k + 1) * P], ident[:, :])
                ins.then_inc(S["ta_done"], 1)

            over = [False]

            def turned_rows(b):
                return KD * b + (KD if over[0] else 2 * KD)

            def results(b):
                pe.wait_ge(S["actt_ready"], b + 1)
                pe.wait_ge(S["fin_act"], 2 * TT)
                at_least(pe, S["ys_ready"], b)
                for k in range(KD):
                    pe.wait_ge(w2_landed[k], 16 * b + 16)
                    for n in range(2):
                        ins = mm(bank(4 + n), actt[:, k, :], w2_ring[:, k, n * HALF:(n + 1) * HALF], start=(k == 0),
                                 stop=(k == KD - 1))
                    if k < KD - 1:
                        ins.then_inc(S["w2_used"], 1)
                ins.then_inc(S["y_done"], 1)
                pe.wait_ge(S["y_done"], b + 1)
                pe.sem_inc(S["w2_used"], 1)

            turn_x(0)
            hidden(0)
            turn_x(1)
            turn_act(0)
            hidden(1)
            with pe.Fori(0, n_more) as i:
                b = i + 2
                turn_x(b)
                results(b - 2)
                turn_act(b - 1)
                hidden(b)
            results(n_more)
            over[0] = True
            turn_act(n_more + 1)
            results(n_more + 1)

        @block.vector
        def _(dve):
            step, settle = order("dve_order")
            V = nc.vector
            dve.wait_ge(S["cols_turned"], 1)
            V.tensor_copy(cols[:, 0:SMALL_ROWS], bank(6)[:, 0:SMALL_ROWS]).then_inc(S["cols_ready"], 1)
            dve.wait_ge(S["c_sig_ready"], 1)
            V.tensor_tensor(c_act, cols[:, C_C:C_C + 8], c_sig, ALU.mult).then_inc(S["c_ready"], 1)
            row0, row1 = cols[:, C_LB:C_LB + 4], cols[:, C_LB + 4:C_LB + 8]
            step(V.tensor_tensor(oml, row0, row1, ALU.max))
            settle(dve)
            V.tensor_tensor(lb0, row0, oml, ALU.subtract).then_inc(S["lb_act"], 1)
            V.tensor_tensor(lb1, row1, oml, ALU.subtract).then_inc(S["lb_act"], 1)

            def rms_factor(dst, root, n):
                dve.wait_ge(S["root_ready"], n)
                step(V.reciprocal(dst, root))
                settle(dve)

            rms_factor(rstd, ssq, 1)
            for t in range(TT):
                V.tensor_scalar(xh[:, t], x_sb[:, t], rstd[:, t:t + 1], None, ALU.mult).then_inc(S["xh_ready"], 1)

            def ada_add(j):
                dve.wait_ge(S["spread_done"], j + 1)
                src = bank(2 + j if j < 4 else 7)
                if j in (4, 5, 10, 11):
                    dst = (g1_b if j < 6 else g2_b)[:, (j % 2) * HALF:(j % 2 + 1) * HALF]
                    dve.wait_ge(S["gate_bias_landed"], 32)
                    V.tensor_tensor(dst, src, dst, ALU.add).then_inc(S["mod_done"], 1)
                else:
                    V.tensor_tensor(mod[:, 4 * j:4 * j + 4], src[:, 0:4], cols[:, 4 * j:4 * j + 4], ALU.add).then_inc(
                        S["mod_done"], 1)

            for j in range(4):
                ada_add(j)
            dve.wait_ge(S["mod_done"], 4)
            V.scalar_tensor_tensor(out=s1c, in0=mod[:, 8:16], scalar=1.0, in1=cols[:, C_N1:C_N1 + 8], op0=ALU.add,
                                   op1=ALU.mult).then_inc(S["mod_done"], 1)
            dve.wait_ge(S["lb_act"], 4)
            step(V.tensor_tensor(lbs, lb0, lb1, ALU.add))
            settle(dve)
            step(V.reciprocal(lbs, lbs))
            settle(dve)
            step(V.tensor_tensor(lb0, lb0, lbs, ALU.mult))
            settle(dve)
            step(V.tensor_scalar(oml, lb0, -1.0, 1.0, ALU.mult, ALU.add))
            settle(dve)

            chunked = lambda a: a.rearrange("p (c s) -> p c s", s=CHUNK)

            def at_chunk(i):
                return chunked(fb[:, :])[:, :, i:i + 1].to_broadcast([P, HEADS * CHUNKS, CHUNK])

            def hg(i):
                done = S["hg_dve"]
                if i == 0:
                    dve.wait_ge(S["evac_act"], 4)
                    for h in range(HEADS):
                        V.tensor_scalar(f3[:, h], f3[:, h], oml[:, h:h + 1], lb0[:, h:h + 1], ALU.mult,
                                        ALU.add).then_inc(done, 1)
                    dve.wait_ge(done, 4)
                    V.tensor_scalar(kb[:, :], fb[:, :], -1.0, 1.0, ALU.mult, ALU.add).then_inc(done, 1)
                elif i == 2:
                    dve.wait_ge(S["hg_act"], 1)
                    V.tensor_tensor_scan(fb[:, :], scan_mask[:, :], ks, 0.0, ALU.mult, ALU.add).then_inc(done, 1)
                    dve.wait_ge(done, 6)
                    V.tensor_tensor(chunked(klt), chunked(fb[:, :]), at_chunk(CHUNK // 2 - 1),
                                    ALU.subtract).then_inc(done, 1)
                elif i == 4:
                    dve.wait_ge(S["hg_act"], 2)
                    dve.wait_ge(S["pads_ready"], 1)
                    dve.wait_ge(S["evac_dve"], 4)
                    qep5 = w1_flat[:, 2048:6144].rearrange("p (n a b s) -> p n a b s", a=2, b=2, s=CHUNK)
                    q4 = qb[:, :].rearrange("p (n a s) -> p n a s", a=2, s=CHUNK)
                    e4 = sr.rearrange("p (n a s) -> p n a s", a=2, s=CHUNK)
                    for a in range(2):
                        V.tensor_tensor(qep5[:, :, a, a, :], q4[:, :, a, :], e4[:, :, a, :], ALU.mult).then_inc(done, 1)
                    dve.wait_ge(S["hg_act"], 3)
                    dve.wait_ge(done, 9)
                    V.tensor_tensor(qb[:, :], qb[:, :], ks, ALU.mult).then_inc(done, 1)
                elif i == 6:
                    dve.wait_ge(S["hg_act"], 4)
                    V.tensor_tensor(ks, kb[:, :], ks, ALU.mult).then_inc(done, 1)
                    V.tensor_tensor(chunked(klt), at_chunk(CHUNK - 1), chunked(fb[:, :]), ALU.subtract).then_inc(done, 1)
                elif i == 8:
                    dve.wait_ge(S["hg_act"], 6)
                    V.tensor_tensor(kb[:, :], kb[:, :], sr, ALU.mult).then_inc(done, 1)
                    V.memset(fb[:, :], 0.0).then_inc(done, 1)

            for u, (kind, i, _, _) in enumerate(UNITS):
                src = bank(u % 3)
                freed = S["evac_dve"]
                if kind == "x":
                    dve.wait_ge(S["proj_done"], u + 1)
                    a = conv_tmp[:, i % 2]
                    w = lambda j: cols[:, C_CW + 8 * j + i:C_CW + 8 * j + i + 1]
                    step(V.tensor_scalar(a, src, w(CONV - 1), cols[:, C_CB + i:C_CB + i + 1], ALU.mult, ALU.add))
                    for d in range(1, CONV):
                        settle(dve)
                        ins = V.scalar_tensor_tensor(out=a[:, d:], in0=src[:, 0:TOK - d], scalar=w(CONV - 1 - d),
                                                     in1=a[:, d:], op0=ALU.mult, op1=ALU.add)
                        if d < CONV - 1:
                            step(ins)
                    ins.then_inc(S["conv_ready"], 1)
                    dve.wait_ge(S["sig_ready"], GATED.index(u) + 1)
                    V.tensor_tensor(xbc[:, i], a, sig_tmp[:, GATED.index(u) % 2], ALU.mult).then_inc(freed, 1)
                elif u in GATED:
                    if u == GATED[-4]:
                        dve.wait_ge(S["hg_dve"], 6)
                    dve.wait_ge(S["sig_ready"], GATED.index(u) + 1)
                    dst = {"q": q3, "g": g3, "z": z3}[kind][:, i]
                    V.tensor_tensor(dst, src, sig_tmp[:, GATED.index(u) % 2], ALU.mult).then_inc(freed, 1)
                elif kind == "dt":
                    dve.wait_ge(S["proj_done"], u + 1)
                    dve.wait_ge(S["bias_landed"], 64)
                    V.tensor_tensor(dtr.rearrange("p (t h) -> p t h", t=TT), src[:, 0:32].rearrange(
                        "p (t h) -> p t h", t=TT), dtb.unsqueeze(1).to_broadcast([P, TT, 8]), ALU.add).then_inc(freed, 1)
                if 7 <= u <= 15:
                    hg(u - 7)
            mask = block_mask[:, :].bitcast(I32)
            for t in range(TT):
                dve.wait_ge(S["att_done"], t + 1)
                for j, a, b in QUARTERS:
                    part = slice(32 * j, 32 * j + 32)
                    V.copy_predicated(att3[part, t].rearrange("p (h s) -> p h s", h=HEADS)[:, :, a:b],
                                      mask[part, a:b].unsqueeze(1).to_broadcast([32, HEADS, b - a]),
                                      bank(3 + t)[part].rearrange("p (h s) -> p h s", h=HEADS)[:, :, a:b]).then_inc(
                        S["att_masked"], 1)

            def state(ch):
                dve.wait_ge(S["ds_done"], ch + 1)
                new, old = sr3[:, (ch + 1) % 4], sr3[:, ch % 4]
                if ch == 0:
                    V.tensor_copy(new, bank(3)).then_inc(S["s_ready"], 1)
                    return
                dve.wait_ge(S["s_ready"], ch)
                if ch >= 3:
                    dve.wait_ge(S["o_done"], (ch - 3) // 2 + 1)
                for h in range(HEADS):
                    hs = slice(h * P, (h + 1) * P)
                    ins = V.scalar_tensor_tensor(out=new[:, hs], in0=old[:, hs], scalar=dec[:, 8 * h + ch:8 * h + ch + 1],
                                                 in1=bank(3 + ch % 4)[:, hs], op0=ALU.mult, op1=ALU.add)
                    if h < HEADS - 1:
                        step(ins)
                ins.then_inc(S["s_ready"], 1)

            def o_norm(t):
                rms_factor(rh[:, 4 * t:4 * t + 4], ssh[:, 4 * t:4 * t + 4], 2 + t)
                for h in range(HEADS):
                    hs = slice(h * P, (h + 1) * P)
                    ins = V.scalar_tensor_tensor(out=g3[:, t, hs], in0=bank(t % 3)[:, hs],
                                                 scalar=rh[:, 4 * t + h:4 * t + h + 1], in1=g3[:, t, hs],
                                                 op0=ALU.mult, op1=ALU.mult)
                    if h < HEADS - 1:
                        step(ins)
                ins.then_inc(S["o_normed"], 1)

            state(0)
            state(1)
            state(2)
            ada_add(4)
            o_norm(0)
            state(3)
            state(4)
            ada_add(5)
            o_norm(1)
            state(5)
            state(6)
            ada_add(6)
            o_norm(2)
            o_norm(3)
            ada_add(7)

            V.scalar_tensor_tensor(out=dt_tmp, in0=dtr, scalar=-1.0, in1=dtr, op0=ALU.mult,
                                   op1=ALU.max).then_inc(S["dt_dve"], 1)
            dve.wait_ge(S["dt_act"], 3)
            step(V.scalar_tensor_tensor(out=dtv, in0=dtr, scalar=0.0, in1=dt_tmp, op0=ALU.max, op1=ALU.add))
            V.tensor_scalar(na, na, -1.0, None, ALU.mult).then_inc(S["dt_dve"], 1)
            settle(dve)
            dve.wait_ge(S["dt_dve"], 2)
            over_t = lambda a: a.rearrange("p (t h) -> p t h", t=TT)
            V.tensor_tensor(over_t(dta), over_t(dtv), na.unsqueeze(1).to_broadcast([P, TT, 8]),
                            ALU.mult).then_inc(S["dt_dve"], 1)
            dve.wait_ge(S["dt_dve"], 3)
            dve.wait_ge(S["acum_done"], 1)
            V.tensor_copy(acum, bank(6)[:, 0:32]).then_inc(S["acum_ready"], 1)
            dve.wait_ge(S["acum_ready"], 1)
            heads = lambda a: a.rearrange("p (h s) -> p h s", h=SSM_HEADS)
            wide = lambda a: a.unsqueeze(2).to_broadcast([P, SSM_HEADS, 64])
            dve.wait_ge(S["o_done"], TT)
            for t in range(TT):
                h8 = slice(8 * t, 8 * t + 8)
                for h in range(SSM_HEADS):
                    ins = V.tensor_scalar(dtri[:, h, :], tri[:, :], dta[:, 8 * t + h:8 * t + h + 1], None, ALU.mult)
                    if h < SSM_HEADS - 1:
                        step(ins)
                ins.then_inc(S["dtri_ready"], 1)
                dve.wait_ge(S["m_copied"], 2 * t + 2)
                step(V.tensor_tensor(heads(xdt), heads(xs), wide(dtv[:, h8]), ALU.mult))
                step(V.tensor_tensor(cbm, bank(1)[:, 256:512].rearrange("p (g t) -> p g t", g=2),
                                     tri[:, :].unsqueeze(1).to_broadcast([P, 2, P]), ALU.mult))
                dve.wait_ge(S["acb_done"], t + 1)
                acb = bank(2, 2).rearrange("p (h t) -> p h t", h=SSM_HEADS)
                for h in range(SSM_HEADS):
                    step(V.tensor_scalar(seg[:, h, :], acb[:, h, :], acum[:, 8 * t + h:8 * t + h + 1], 0.0,
                                         ALU.subtract, ALU.min))
                step(V.tensor_copy(last, acb[:, :, P - 1]))
                settle(dve)
                V.tensor_tensor(wgt, last, acum[:, h8], ALU.subtract).then_inc(S["m_seg"], 1)
                dve.wait_ge(S["m_exp"], 3 * t + 3)
                for g in range(2):
                    step(V.tensor_tensor(seg[:, 4 * g:4 * g + 4, :], seg[:, 4 * g:4 * g + 4, :],
                                         cbm[:, g:g + 1, :].to_broadcast([P, 4, P]), ALU.mult))
                settle(dve)
                V.tensor_tensor(heads(xw), heads(xdt), wide(wgt), ALU.mult).then_inc(S["m_ready"], 1)
                ada_add(8 + t)
                step(V.tensor_tensor(heads(yt), heads(xs), wide(skip), ALU.mult))
                settle(dve)
                dve.wait_ge(S["my_done"], t + 1)
                step(V.tensor_tensor(yt, yt, bank(4), ALU.add))
                if t == 0:
                    step(V.tensor_copy(sm, bank(6)))
                    settle(dve)
                else:
                    dve.wait_ge(S["ea_ready"], 1)
                    step(V.tensor_tensor(heads(m_tmp), heads(bank(5)), wide(ea[:, h8]), ALU.mult))
                    step(V.tensor_tensor(heads(sm), heads(sm), wide(eal), ALU.mult))
                    settle(dve)
                    step(V.tensor_tensor(yt, yt, m_tmp, ALU.add))
                    step(V.tensor_tensor(sm, sm, bank(6), ALU.add))
                    settle(dve)
                V.tensor_tensor(z3[:, t], z3[:, t], yt, ALU.mult).then_inc(S["m_gated"], 1)
                rms_factor(rh[:, 2 * t:2 * t + 2], ssh[:, 2 * t:2 * t + 2], 6 + t)
                step(V.tensor_scalar(z3[:, t, 0:256], z3[:, t, 0:256], rh[:, 2 * t:2 * t + 1], None, ALU.mult))
                settle(dve)
                V.tensor_scalar(z3[:, t, 256:512], z3[:, t, 256:512], rh[:, 2 * t + 1:2 * t + 2], None,
                                ALU.mult).then_inc(S["y_ready"], 1)
                dve.wait_ge(S["y_ready"], t + 1)
                V.tensor_copy(m_tmp[:, 0:8], acum[:, 0:8]).then_inc(S["m_free"], 1)
            step(V.scalar_tensor_tensor(out=s2c, in0=mod[:, 32:40], scalar=1.0, in1=cols[:, C_N2:C_N2 + 8],
                                        op0=ALU.add, op1=ALU.mult))
            settle(dve)
            for u in range(2 * TT):
                h, t = u // TT, u % TT
                hs = slice(h * HALF, (h + 1) * HALF)
                dve.wait_ge(S["mix_done"], u + 1)
                tmp = (m_tmp, m_junk)[u % 2]
                at_least(dve, S["x2_ready"], u - 1)
                step(V.tensor_tensor(tmp, bank(4 + u % 4), g1_b[:, hs], ALU.mult))
                settle(dve)
                V.tensor_tensor(x_sb[:, t, hs], x_sb[:, t, hs], tmp, ALU.add).then_inc(S["x2_ready"], 1)
            rms_factor(rstd, ssq, 10)
            for t in range(TT):
                V.tensor_scalar(xh[:, t], x_sb[:, t], rstd[:, t:t + 1], None, ALU.mult).then_inc(S["xh2_ready"], 1)

            dve.wait_ge(S["logits_done"], 1)
            dve.wait_ge(S["xh2_stored"], 16 * TT)
            dve.wait_ge(S["iota_ready"], 1)
            step(V.tensor_tensor(logits, bank(4)[:, 0:128].rearrange("p (t e) -> p t e", t=TT),
                                 rb.unsqueeze(1).to_broadcast([P, TT, EXPERTS]), ALU.add))
            settle(dve)
            for t in range(TT):
                step(V.max(top8[:, 8 * t:8 * t + 8], logits[:, t, :]))
            settle(dve)
            for t in range(TT):
                step(V.max_index(idx8[:, 8 * t:8 * t + 8], top8[:, 8 * t:8 * t + 8], logits[:, t, :]))
            settle(dve)
            by8 = lambda a: a.rearrange("p (t k) -> p t k", t=TT)
            step(V.tensor_copy(idx8f, idx8))
            V.tensor_tensor(by8(gate_e), by8(top8)[:, :, 0:TOP], by8(top8)[:, :, 0:1].to_broadcast([P, TT, TOP]),
                            ALU.subtract).then_inc(S["route_act"], 1)
            settle(dve)
            hot4 = onehot.rearrange("p (t k e) -> p t k e", t=TT, k=TOP)
            hotp4 = onehot_p.rearrange("p (t k e) -> p t k e", t=TT, k=TOP)
            for t in range(TT):
                step(V.tensor_tensor(hot4[:, t], iota[:, 0:EXPERTS].unsqueeze(1).to_broadcast([P, TOP, EXPERTS]),
                                     by8(idx8f)[:, t, 0:TOP].unsqueeze(2).to_broadcast([P, TOP, EXPERTS]),
                                     ALU.is_equal))
            settle(dve)
            step(V.tensor_tensor(member, hot4[:, :, 0, :], hot4[:, :, 1, :], ALU.add))
            settle(dve)
            step(V.tensor_tensor(member, member, hot4[:, :, 2, :], ALU.add))
            settle(dve)
            V.tensor_tensor(member, member, hot4[:, :, 3, :], ALU.add).then_inc(S["route_pe"], 1)
            dve.wait_ge(S["route_pe"], 1)
            for r in range(3):
                ins = V.tensor_copy(member3[:, :, r, :], member)
                if r < 2:
                    step(ins)
            ins.then_inc(S["route_pe"], 1)
            dve.wait_ge(S["route"], 2)
            V.tensor_tensor(more[0:96, :], bank(1)[0:96, 0:1], thr[0:96, :], ALU.is_gt).then_inc(S["route_pe"], 1)
            dve.wait_ge(S["route"], 3)
            step(V.tensor_copy(more_pos, bank(2)[:, 0:1]))
            step(V.tensor_scalar(tab_n, bank(2)[0:1, 1:2], float(EXPERTS - 2), None, ALU.add))
            settle(dve)
            V.tensor_scalar(ext_hot[0:96, :], iota[0:96, 0:EXTRA], more_pos[0:96, :], more[0:96, :], ALU.is_equal,
                            ALU.mult).then_inc(S["route_pe"], 1)
            dve.wait_ge(S["route_act"], 2)
            step(V.tensor_reduce(gate_s, by8(gate_e), AX_X, ALU.add))
            settle(dve)
            step(V.reciprocal(gate_r, gate_s))
            settle(dve)
            step(V.tensor_tensor(by8(gates), by8(gate_e), gate_r.unsqueeze(2).to_broadcast([P, TT, TOP]), ALU.mult))
            settle(dve)
            for t in range(TT):
                step(V.tensor_tensor(hotp4[:, t], hot4[:, t],
                                     by8(gates)[:, t, :].unsqueeze(2).to_broadcast([P, TOP, EXPERTS]), ALU.mult))
            settle(dve)
            step(V.tensor_tensor(gate_dense, hotp4[:, :, 0, :], hotp4[:, :, 1, :], ALU.add))
            settle(dve)
            step(V.tensor_tensor(gate_dense, gate_dense, hotp4[:, :, 2, :], ALU.add))
            settle(dve)
            V.tensor_tensor(gate_dense, gate_dense, hotp4[:, :, 3, :], ALU.add).then_inc(S["route_pe"], 1)
            dve.wait_ge(S["route_pe"], 5)
            dve.wait_ge(S["route"], 5)
            step(V.tensor_copy(pos, bank(0)[:, 0:128]))
            settle(dve)
            for t in range(TT):
                step(V.tensor_tensor(hotp4[:, t], hot4[:, t],
                                     pos[:, 32 * t:32 * t + 32].unsqueeze(1).to_broadcast([P, TOP, EXPERTS]), ALU.mult))
            settle(dve)
            step(V.tensor_reduce(pos_k, onehot_p.rearrange("p (n e) -> p n e", e=EXPERTS), AX_X, ALU.add))
            settle(dve)
            step(V.tensor_scalar(hi1, pos_k, float(P), None, ALU.is_ge))
            step(V.tensor_scalar(hi2, pos_k, float(2 * P), None, ALU.is_ge))
            step(V.tensor_scalar(hi, pos_k, float(3 * P), None, ALU.is_ge))
            settle(dve)
            step(V.tensor_tensor(hi1, hi1, hi2, ALU.add))
            settle(dve)
            step(V.tensor_tensor(hi, hi, hi1, ALU.add))
            settle(dve)
            step(V.scalar_tensor_tensor(out=lo, in0=hi, scalar=-float(P), in1=pos_k, op0=ALU.mult, op1=ALU.add))
            step(V.scalar_tensor_tensor(out=by8(key), in0=by8(hi), scalar=float(EXPERTS), in1=by8(idx8f)[:, :, 0:TOP],
                                        op0=ALU.mult, op1=ALU.add))
            step(V.tensor_copy(gates_t, bank(7)[0:EXPERTS, :]))
            settle(dve)
            V.tensor_copy(tab_f[:, :, EXPERTS:BLOCKS], bank(3)[:, 0:2 * EXTRA].rearrange(
                "p (a b) -> p a b", a=2)).then_inc(S["route_pe"], 1)
            dve.wait_ge(S["route_pe"], 6)
            for n in range(TT * TOP):
                if n >= 2:
                    dve.wait_ge(S["route"], 5 + n - 1)
                one = slice(n, n + 1)
                step(V.tensor_scalar(lo_hot[:, n % 2, :], iota, lo[:, one], None, ALU.is_equal))
                step(V.tensor_scalar(key_hot[:, n % 2, 0:P], iota, key[:, one], tok_id[:, one], ALU.is_equal, ALU.mult))
                settle(dve)
                V.tensor_scalar(key_hot[:, n % 2, P:2 * P], iota, key[:, one], gates[:, one], ALU.is_equal,
                                ALU.mult).then_inc(S["route_pe"], 1)
            dve.wait_ge(S["route"], 5 + TT * TOP)
            step(V.tensor_scalar(slot_tok, bank(4)[:, 0:P], float(UNUSED), None, ALU.add))
            step(V.tensor_copy(slot_gate, bank(4)[:, P:2 * P]))
            step(V.tensor_copy(tab[:, 0:2 * BLOCKS], tab_f[0:1, :, :].rearrange("p a b -> p (a b)")))
            step(V.tensor_scalar(blk_hot, tab_f[:, 0, :], mod32, None, ALU.is_equal))
            settle(dve)
            V.tensor_copy(pos[:, 0:1], thr).then_inc(S["tables_ready"], 1)
            dve.wait_ge(S["tables_ready"], 1)
            n_more = dve.value_load(tab_n, min_val=EXPERTS - 2, max_val=MAX_BLOCKS - 2)

            def modulated(b):
                dve.wait_ge(S["tx_done"], b + 1)
                for k in range(KD):
                    V.tensor_scalar(xgt[:, k, :], bank(6, 2)[:, k * P:(k + 1) * P], s2c[:, k:k + 1],
                                    mod[:, 24 + k:25 + k], ALU.mult, ALU.add).then_inc(S["xgt_ready"], 1)

            def pick(b):
                at_least(dve, S["w1_used"], KD * b)
                hot = blk_hot[0:96, bass.ds(b, 1)] if not isinstance(b, int) else blk_hot[0:96, b:b + 1]
                V.tensor_scalar(sel[0:96, :], tri_ones, hot, None, ALU.mult).then_inc(S["sel_ready"], 1)

            tri_ones = iota[0:96, :]

            def swiglu(b):
                dve.wait_ge(S["w1_used"], KD * b + KD)
                V.tensor_scalar(glu, bank(0, 2), LIMIT, None, ALU.min).then_inc(S["clipped"], 1)
                V.tensor_scalar(lin, bank(2, 2), LIMIT, -LIMIT, ALU.min, ALU.max).then_inc(S["clipped"], 1)
                dve.wait_ge(S["clipped"], 2 * b + 2)
                V.scalar_tensor_tensor(out=lin, in0=lin, scalar=1.0, in1=glu, op0=ALU.add, op1=ALU.mult).then_inc(
                    S["lin_ready"], 1)
                dve.wait_ge(S["lin_ready"], b + 1)
                dve.wait_ge(S["sig2_ready"], b + 1)
                V.tensor_tensor(act_sb, lin, sg, ALU.mult).then_inc(S["act_ready"], 1)

            step(V.memset(iota, 1.0))
            settle(dve)
            modulated(0)
            pick(0)
            modulated(1)
            pick(1)
            swiglu(0)
            with dve.Fori(0, n_more) as i:
                b = i + 2
                modulated(b)
                pick(b)
                swiglu(b - 1)
            swiglu(n_more + 1)

            for t in range(TT):
                dve.wait_ge(S["moe_landed"], 16 * (t + 1))
                step(V.tensor_tensor(xh[:, t], xh[:, t], g2_b[:, :], ALU.mult))
                settle(dve)
                V.tensor_tensor(x_sb[:, t], x_sb[:, t], xh[:, t], ALU.add).then_inc(S["fin"], 1)
            rms_factor(rstd, ssq, 11)
            dve.wait_ge(S["fnw_landed"], 16)
            for t in range(TT):
                V.scalar_tensor_tensor(out=x_sb[:, t], in0=x_sb[:, t], scalar=rstd[:, t:t + 1], in1=fnw,
                                       op0=ALU.mult, op1=ALU.mult).then_inc(S["out_ready"], 1)


_INS = ['x', 'c', 'ada_w', 'ada_b', 'norm1_w', 'w_in', 'hg_lb_logits', 'hg_norm_w', 'ssm_a_log', 'ssm_dt_bias',
        'ssm_d', 'ssm_conv_w', 'ssm_conv_b', 'ssm_norm_w', 'w_out', 'norm2_w', 'router_w', 'router_b',
        'exp_w1', 'exp_b1', 'exp_w2', 'exp_b2', 'final_norm_w']
_OUTS = [((1, 512, 1024), 'float32')]


def kernel(**inputs):
    import numpy as _np
    import concourse.bacc as _bacc
    from concourse import mybir as _mybir
    from concourse.bass_utils import run_bass_kernel_spmd as _run

    nc = _bacc.Bacc("TRN2", target_bir_lowering=False, num_devices=1)
    arrays, args = {}, []
    for name in _INS:
        a = _np.ascontiguousarray(inputs[name])
        arrays[f"in_{name}_dram"] = a
        args.append(nc.dram_tensor(f"in_{name}_dram", a.shape, _mybir.dt.from_np(a.dtype), kind="ExternalInput").ap())
    for i, (shape, dtype) in enumerate(_OUTS):
        dt = _mybir.dt.from_np(_np.dtype(dtype))
        args.append(nc.dram_tensor(f"out_{i}_dram", shape, dt, kind="ExternalOutput").ap())
    build(nc, *args)
    r = _run(nc, [arrays], core_ids=[0])
    got = tuple(r.results[0][f"out_{i}_dram"] for i in range(len(_OUTS)))
    return got[0]
```

```python
from contextlib import ExitStack

import concourse.bass as bass
from concourse import mybir

F32 = mybir.dt.float32
F32R = mybir.dt.float32r
BF16 = mybir.dt.bfloat16
I32 = mybir.dt.int32
U32 = mybir.dt.uint32
ALU = mybir.AluOpType
ACT = mybir.ActivationFunctionType
AX_X = mybir.AxisListType.X

P = 128
D = 1024
KD = D // P
TOK = 512
TT = TOK // P
EPS = 1e-6
HEADS = 4
HG = 512
CHUNK = 64
CHUNKS = TOK // CHUNK
SSM_HEADS = 8
CONV = 4
EXPERTS = 32
TOP = 4
FF = 1024
LIMIT = 7.0
ALPHA = 1.702
HALF = 512
EXTRA = 16
UNITS_W1, UNITS_W2 = 8, 4
RAW, PARTS = 6, 4
BLOCKS = EXPERTS + EXTRA
MAX_BLOCKS = EXPERTS + (TOK * TOP - EXPERTS) // P
SLOT_GROUPS = TOK // P
UNUSED = TOK

C_ADAB, C_N1, C_N2, C_CW, C_CB, C_LB, C_HGN, C_SSMN, C_C = 0, 48, 56, 64, 96, 104, 112, 113, 117
SMALL_ROWS = 125

QUARTERS = [(j, CHUNK * (j // 2) + 32 * (j % 2), CHUNK * (j // 2) + CHUNK) for j in range(4)]

Q_COL, F_COL, I_COL, G_COL, Z_COL, X_COL, DT_COL = 0, 512, 1024, 1536, 2048, 2560, 3584
LOADS = ([("ada", j) for j in range(4)]
         + [("in", c) for c in (Q_COL, F_COL, I_COL, G_COL, X_COL, X_COL + HALF, Z_COL)]
         + [("ada", j) for j in range(4, 12)] + [("out", 0), ("out", 1)])
L_IN, L_ADA2, L_OUT = 4, 11, 19

UNITS = ([("q", i, L_IN, "dve") for i in range(4)] + [("f", i, L_IN + 1, "act") for i in range(4)]
         + [("i", i, L_IN + 2, "act") for i in range(4)] + [("g", i, L_IN + 3, "dve") for i in range(4)]
         + [("x", i, L_IN + 4 + i // 4, "dve") for i in range(8)] + [("dt", 0, None, "dve")]
         + [("z", i, L_IN + 6, "dve") for i in range(4)])


def evacuated(u):
    who = UNITS[u][3]
    return who, sum(x[3] == who for x in UNITS[:u + 1])


GATED = [u for u, x in enumerate(UNITS) if x[0] in ("q", "g", "z", "x")]


def gated_done(n):
    return evacuated(GATED[n])[1]


def build(nc, x, c, ada_w, ada_b, norm1_w, w_in, hg_lb_logits, hg_norm_w, ssm_a_log, ssm_dt_bias,
          ssm_d, ssm_conv_w, ssm_conv_b, ssm_norm_w, w_out, norm2_w, router_w, router_b,
          exp_w1, exp_b1, exp_w2, exp_b2, final_norm_w, out):
    with ExitStack() as ctx:
        def sb(name, shape, dt=F32):
            return ctx.enter_context(nc.sbuf_tensor(name, shape, dt))

        def sem(name):
            return ctx.enter_context(nc.semaphore(name))

        psum = ctx.enter_context(nc.psum_tensor("banks", [P, 8 * HALF], F32))

        def bank(b, n=1):
            return psum[:, b * HALF:(b + n) * HALF]

        rows_dram = nc.dram_tensor("moe_input_rows", [TOK, D], F32, kind="Internal").ap()
        moe_dram = nc.dram_tensor("moe_rows", [TOK, D], F32, kind="Internal").ap()

        KIB = 1024
        base = -(-nc.sbuf_base // 32) * 32
        arena = ctx.enter_context(nc.sbuf_tensor("arena", [P, 180 * 256], F32))

        def place(name, shape, kib, dt=F32):
            return nc.alloc_sbuf_tensor_at(name, shape, dt, offset=base + int(kib * KIB))

        mixer = place("mixer", [P, 16384], 0)
        window = place("window", [P, 2, KD, HALF], 64)
        x_sb = sb("x_sb", [P, TT, D])
        g1_b = place("g1_b", [P, D], 176)
        g2_b = sb("g2_b", [P, D])
        ht = place("ht", [P, KD, TOK], 96)
        xc = place("xc", [P, KD * TOK], 112)
        qb, fb, kb, vb, gb, zb = (place(n, [P, 2048], 128 + 8 * i)
                                  for i, n in enumerate(("qb", "fb", "kb", "vb", "gb", "zb")))
        ident = sb("ident", [P, P])
        tri = sb("tri", [P, P])
        ones = sb("ones", [P, P])
        block_mask = sb("block_mask", [P, P])
        cols = sb("cols", [P, P])
        row = sb("row", [P, HALF])
        rw = sb("rw", [P, KD, EXPERTS])
        misc = sb("misc", [P, 560])
        c_pad = rw

        at = [0]

        def small(n, parts=P):
            a = at[0]
            at[0] += n
            assert at[0] <= 560
            return misc[0:parts, a:a + n]

        win = window
        w1_flat = mixer[:, :]
        ks = w1_flat[:, 0:2048]
        qep = w1_flat[:, 2048:6144].rearrange("p (h c s) -> p h c s", h=HEADS, c=CHUNKS)
        vp = w1_flat[:, 6144:10240].rearrange("p (c n) -> p c n", c=CHUNKS)
        sr = w1_flat[:, 10240:12288]
        klt = w1_flat[:, 12288:14336]
        sig_tmp = w1_flat[:, 14336:15360].rearrange("p (b n) -> p b n", b=2)
        conv_tmp = w1_flat[:, 15360:16384].rearrange("p (b n) -> p b n", b=2)
        small_rows = ks[0:SMALL_ROWS, 0:P]
        scan_mask = zb

        xh = xc[:, :].rearrange("p (t d) -> p t d", t=TT)
        xbc = xc[:, :].rearrange("p (k t) -> p k t", k=KD)

        def by_head(a):
            return a.rearrange("p (h t) -> p h t", h=HEADS)

        def by_tile(a):
            return a.rearrange("p (t n) -> p t n", t=TT)

        q3, f3, k3, ks3 = by_head(qb[:, :]), by_head(fb[:, :]), by_head(kb[:, :]), by_head(ks)
        v3, g3, z3, att3, klt3, sr3 = (by_tile(a) for a in (vb[:, :], gb[:, :], zb[:, :], fb[:, :], klt, sr))

        mod = small(48)
        s1c, s2c, c_sig = small(8), small(8), small(8)
        lb0, lb1, lbs, oml = small(4), small(4), small(4), small(4)
        ssq, rstd = small(4), small(4)
        dec = small(32)
        ssh, rh = small(16), small(16)
        dtb, alog, skip = small(8), small(8), small(8)
        dtr, dtv, dta, dt_tmp, acum, ea = (small(32) for _ in range(6))
        na = small(8)
        last, wgt, eal = small(8), small(8), small(8)
        wdt = small(64).rearrange("p (k n) -> p k n", k=KD)
        rb = small(32)
        eps = small(1)

        S = {n: sem(n) for n in (
            "pool_order", "dve_order", "act_order", "consts_ready", "pads_ready", "small_landed", "x_landed",
            "bias_landed", "gate_bias_landed", "dt_w_landed", "cols_turned", "cols_ready", "c_sig_ready",
            "c_ready", "row_done", "row_copied", "spread_done", "mod_done", "sq_ready", "root_ready", "xh_ready",
            "xt_done", "ht_ready", "win_used", "proj_done", "evac_act", "evac_dve", "sig_ready",
            "conv_ready", "hg_dve", "hg_act", "lb_act", "att_done", "att_masked", "klt_turned",
            "klt_ready", "vp_ready", "ds_done", "s_ready", "o_done", "o_sq", "o_normed",
            "dt_dve", "dt_act", "acum_done", "acum_ready", "ea_ready", "m_turned", "dtri_ready", "acb_done",
            "m_copied", "m_seg", "m_exp", "m_ready", "my_done", "m_free", "m_gated", "m_sq", "y_ready",
            "mt_turned", "mt_ready", "mix_done", "x2_ready", "sq2_ready", "xh2_ready",
            "rows_turned", "rows_ready", "rows_stored",
            "xt2_done", "ht2_ready", "rw_landed", "logits_done", "b1_landed", "b1_ready", "b2_landed",
            "iota_ready", "route", "route_pe", "route_act", "tables_ready", "moe_init", "moe_stored",
            "stage", "dma_go", "xg_landed", "tx_done", "x_hi_ready", "xgt_ready", "sel_ready", "hi_done", "lo_done",
            "w_used", "clipped", "lin_ready", "sig2_ready", "act_ready", "ta_done", "a_hi_ready", "actt_ready",
            "ys_ready", "scattered", "fin", "fin_act", "fnw_landed", "out_ready", "out_stored")}
        win_landed = [sem(f"win_landed{i}") for i in range(2)]
        moe_landed = [sem(f"moe_landed{t}") for t in range(TT)]
        raw_landed = [sem(f"raw_landed{i}") for i in range(RAW)]

        xs, xdt, xw, yt = (qb[:, i * 512:(i + 1) * 512] for i in range(4))
        seg = kb[:, 0:1024].rearrange("p (h t) -> p h t", h=SSM_HEADS)
        dtri = kb[:, 1024:2048].rearrange("p (h t) -> p h t", h=SSM_HEADS)
        btk = vb[:, 0:256]
        cbm = vb[:, 256:512].rearrange("p (g t) -> p g t", g=2)
        sm = vb[:, 512:1024]
        m_tmp = vb[:, 1024:1536]
        m_junk = vb[:, 1536:2048]

        o = [0]

        def cut(n):
            a = o[0]
            o[0] += n
            assert o[0] <= 4096
            return xc[:, a:a + n]

        onehot, onehot_p = cut(512), cut(512)
        member = cut(128).rearrange("p (t e) -> p t e", t=TT)
        member3 = cut(384).rearrange("p (t r e) -> p t r e", t=TT, r=3)
        lo_hot = cut(256).rearrange("p (b s) -> p b s", b=2)
        key_hot = cut(512).rearrange("p (b n) -> p b n", b=2)
        b2_sb = cut(1024)[0:EXPERTS, :]
        gates_t = cut(512)[0:EXPERTS, :]
        logits = cut(128).rearrange("p (t e) -> p t e", t=TT)
        gate_dense = cut(128).rearrange("p (t e) -> p t e", t=TT)
        o2 = [0]

        def cut2(n, dt=None):
            a = o2[0]
            o2[0] += n
            assert o2[0] <= 2048
            v = qb[:, a:a + n]
            return v.bitcast(dt) if dt is not None else v

        top8, idx8f = cut2(32), cut2(32)
        idx8 = cut2(32, U32)
        gate_e, gate_s, gate_r, gates = cut2(16), cut2(4), cut2(4), cut2(16)
        pos, pos_k, hi1, hi2, hi, lo, key = cut2(128), cut2(16), cut2(16), cut2(16), cut2(16), cut2(16), cut2(16)
        more, more_pos, ext_hot = cut2(1), cut2(1), cut2(16)
        iota = cut2(128)
        tris = cut2(128)
        tok_id, thr, col_q, mod32 = cut2(16), cut2(1), cut2(1), cut2(1)
        col_bc, mod_bc = cut2(128), cut2(128)
        tab_f = cut2(2 * BLOCKS).rearrange("p (a b) -> p a b", a=2)
        slot_tok = row[:, 0:P].bitcast(I32)
        slot_gate = row[:, P:2 * P]
        blk_hot = row[:, 256:256 + BLOCKS]
        tab = row[0:1, 304:304 + 2 * BLOCKS + 1].bitcast(I32)
        tab_e, tab_col, tab_n = tab[:, 0:BLOCKS], tab[:, BLOCKS:2 * BLOCKS], tab[:, 2 * BLOCKS:2 * BLOCKS + 1]
        stage_g = row[:, 408:409].bitcast(I32)
        stage_s = row[:, 409:410].bitcast(I32)

        raw = [place(f"raw{i}", [P, 2048], 8 * i) for i in range(RAW)]
        w_hi = [place(f"w_hi{i}", [P, 2048], 64 + 8 * i, F32R) for i in range(PARTS)]
        w_lo = [place(f"w_lo{i}", [P, 2048], kib, F32R) for i, kib in enumerate((48, 56, 136, 144))]
        xg = vb[:, 0:1024]
        x_hi = place("x_hi", [P, KD, P], 132, F32R)
        x_lo = place("x_lo", [P, KD, P], 176, F32R)
        a_hi = place("a_hi", [P, KD, P], 112, F32R)
        a_lo = place("a_lo", [P, KD, P], 116, F32R)
        glu, lin = gb[:, 0:1024], gb[:, 1024:2048]
        act_sb = ht[:, 4:6, :].rearrange("p k t -> p (k t)")
        ys, sg = ht[:, 0:2, :].rearrange("p k t -> p (k t)"), ht[:, 2:4, :].rearrange("p k t -> p (k t)")
        flat = lambda a: a.rearrange("p k s -> p (k s)")
        sel = ones[:, 0:64].bitcast(BF16)
        b1_raw = kb[:, :]
        h2_rows = [gb[:, 0:D], gb[:, D:2 * D], vb[:, D:2 * D], g1_b[:, :]]
        b1_parts = zb[:, 0:1024].bitcast(BF16)
        fnw = zb[:, 1024:2048]

        def order(name):
            n = [0]

            def step(ins):
                n[0] += 1
                ins.then_inc(S[name], 1)

            def settle(eng):
                eng.wait_ge(S[name], n[0])

            return step, settle

        LOOPED = UNITS_W2 + UNITS_W1

        def unit(i, j):
            return LOOPED * i + (2 * UNITS_W1 + j)

        def landings(i, j):
            return (LOOPED // RAW) * i + ((2 * UNITS_W1 + j) // RAW + 1)

        block = ctx.enter_context(nc.Block())

        def at_least(eng, s, value):
            if not isinstance(value, int) or value > 0:
                eng.wait_ge(s, value)

        @block.sync
        def _(sp):
            rows = lambda a, n: a.rearrange("a (k p) -> (a k) p", p=P)
            r0 = 0
            for src in (rows(ada_b, 48), rows(norm1_w, 8), rows(norm2_w, 8),
                        ssm_conv_w[0].rearrange("j (k p) -> (j k) p", p=P), rows(ssm_conv_b, 8),
                        hg_lb_logits.rearrange("l (k p) -> (l k) p", p=P), hg_norm_w, rows(ssm_norm_w, 4),
                        rows(c, 8)):
                n = src.shape[0]
                sp.dma_start(small_rows[r0:r0 + n, :], src).then_inc(S["small_landed"], 16)
                r0 += n
            assert r0 == SMALL_ROWS
            xv = x[0].rearrange("(t p) d -> p t d", p=P)
            sp.dma_start(x_sb[:, :, :], xv).then_inc(S["x_landed"], 16)
            ada_v = ada_w[0].rearrange("(k p) n -> p k n", p=P)
            in_v = w_in[0].rearrange("(k p) n -> p k n", p=P)
            out_v = w_out[0].rearrange("(k p) n -> p k n", p=P)
            for n, (kind, j) in enumerate(LOADS):
                if n >= 2:
                    sp.wait_ge(S["win_used"], n - 1)
                src = ada_v if kind == "ada" else in_v if kind == "in" else out_v
                a = j if kind == "in" else j * HALF
                sp.dma_start(win[:, n % 2], src[:, :, a:a + HALF]).then_inc(win_landed[n % 2], 16)
                if n == 4:
                    for dst, src in ((dtb, ssm_dt_bias), (alog, ssm_a_log), (skip, ssm_d), (rb, router_b)):
                        sp.dma_start(dst, src[0].partition_broadcast(P)).then_inc(S["bias_landed"], 16)
                    sp.dma_start(wdt, in_v[:, :, DT_COL:DT_COL + 8]).then_inc(S["dt_w_landed"], 16)
                    for dst, a in ((g1_b, 2 * D), (g2_b, 5 * D)):
                        sp.dma_start(dst[:, :], ada_b[0, a:a + D].partition_broadcast(P)).then_inc(
                            S["gate_bias_landed"], 16)

            sp.wait_ge(S["row_done"], 12)
            sp.dma_start(rw[:, :, :], router_w[0].rearrange("(k p) n -> p k n", p=P)).then_inc(S["rw_landed"], 16)

            def load(src, n, slot):
                at_least(sp, S["lo_done"], n - RAW + 1)
                sp.dma_start(src_tile(raw[slot], src), src).then_inc(raw_landed[slot], 16)

            def src_tile(tile, src):
                return tile[:, :] if len(src.shape) == 2 else tile[:, :].rearrange("p (k n) -> p k n", k=2)

            def w1_rows(e, k):
                return exp_w1[0, e, k * P:(k + 1) * P, :]

            def w2_rows(e, k):
                return exp_w2[0, e, 2 * k * P:2 * (k + 1) * P, :].rearrange("(k p) n -> p k n", p=P)

            sp.wait_ge(S["o_normed"], TT)
            for k in range(RAW):
                load(w1_rows(0, k), k, k)
            sp.wait_ge(S["xt2_done"], KD)
            for i in range(3):
                sp.dma_start(b1_raw[32 * i:32 * i + 32, :], exp_b1[0]).then_inc(S["b1_landed"], 16)
            sp.dma_start(b2_sb, exp_b2[0]).then_inc(S["b2_landed"], 16)
            EARLY = 3
            for n in range(RAW, RAW + EARLY):
                load(w1_rows(n // UNITS_W1, n % UNITS_W1), n, n % RAW)
            for t in range(TT):
                sp.wait_ge(S["rows_ready"], t + 1)
                sp.dma_start(rows_dram[t * P:(t + 1) * P, :], h2_rows[t]).then_inc(S["rows_stored"], 16)
            sp.dma_start(fnw, final_norm_w.partition_broadcast(P)).then_inc(S["fnw_landed"], 16)
            for n in range(RAW + EARLY, 2 * UNITS_W1):
                load(w1_rows(n // UNITS_W1, n % UNITS_W1), n, n % RAW)
            sp.wait_ge(S["tables_ready"], 1)
            n_more = sp.value_load(tab_n, min_val=EXPERTS - 3, max_val=MAX_BLOCKS - 3)

            def load_turn(i):
                e = sp.value_load(tab_e[:, bass.ds(i + 2, 1)], min_val=0, max_val=EXPERTS - 1)
                e_before = sp.value_load(tab_e[:, bass.ds(i, 1)], min_val=0, max_val=EXPERTS - 1)
                for j in range(LOOPED):
                    src = w2_rows(e_before, j) if j < UNITS_W2 else w1_rows(e, j - UNITS_W2)
                    load(src, unit(i, j), (2 * UNITS_W1 + j) % RAW)

            with sp.Fori(0, n_more) as i:
                load_turn(i)
            load_turn(n_more)
            for j in range(2 * UNITS_W2):
                if j % UNITS_W2 == 0:
                    e = sp.value_load(tab_e[:, bass.ds(n_more + (1 + j // UNITS_W2), 1)], min_val=0,
                                      max_val=EXPERTS - 1)
                load(w2_rows(e, j % UNITS_W2), unit(n_more + 1, j), (2 * UNITS_W1 + j) % RAW)
            sp.wait_ge(S["scattered"], n_more * 16 + 48)
            for t in range(TT):
                sp.dma_start(xh[:, t], moe_dram[t * P:(t + 1) * P, :]).then_inc(moe_landed[t], 16)
            for t in range(TT):
                sp.wait_ge(S["out_ready"], t + 1)
                sp.dma_start(out[0, t * P:(t + 1) * P, :], x_sb[:, t]).then_inc(S["out_stored"], 16)
            sp.wait_ge(S["out_stored"], 16 * TT)

        @block.gpsimd
        def _(pool):
            step, settle = order("pool_order")
            step(pool.memset(ident[:, :], 0.0))
            step(pool.memset(eps, EPS))
            step(pool.memset(c_pad[:, :, :], 0.0))
            step(pool.memset(tri[:, :], 1.0))
            step(pool.memset(block_mask[:, :], 1.0))
            step(pool.memset(ones[:, :], 1.0))
            step(pool.memset(scan_mask[:, :], 1.0))
            settle(pool)
            step(pool.affine_select(out=ident[:, :], in_=ident[:, :], compare_op=ALU.not_equal, fill=1.0, base=0,
                                    pattern=[[-1, P]], channel_multiplier=1))
            for m in (tri, block_mask):
                step(pool.affine_select(out=m[:, :], in_=m[:, :], compare_op=ALU.is_ge, fill=0.0, base=0,
                                        pattern=[[1, P]], channel_multiplier=-1))
            step(pool.memset(scan_mask[:, :].rearrange("p (c s) -> p c s", s=CHUNK)[:, :, 0:1], 0.0))
            settle(pool)
            pool.memset(block_mask[0:64, 64:128], 0.0).then_inc(S["consts_ready"], 1)
            step(pool.memset(qep, 0.0))
            settle(pool)
            pool.memset(vp, 0.0).then_inc(S["pads_ready"], 1)
            pool.wait_ge(S["pads_ready"], 1)
            pool.wait_ge(S["evac_act"], 8)
            vp4 = vp.rearrange("p (t a) n -> p t a n", a=2)
            pool.tensor_copy(vp4[0:64, :, 0, :], v3[0:64]).then_inc(S["vp_ready"], 1)
            pool.tensor_copy(vp4[64:128, :, 1, :], v3[64:128]).then_inc(S["vp_ready"], 1)

            pool.wait_ge(S["y_ready"], TT)
            step(pool.iota(iota, pattern=[[1, P]], base=0, channel_multiplier=0, allow_small_or_imprecise_dtypes=True))
            step(pool.memset(tris, 1.0))
            step(pool.iota(tok_id, pattern=[[P, TT], [0, TOP]], base=-UNUSED, channel_multiplier=1,
                           allow_small_or_imprecise_dtypes=True))
            step(pool.iota(col_q, pattern=[[0, 1]], base=EXPERTS, channel_multiplier=1,
                           allow_small_or_imprecise_dtypes=True))
            step(pool.iota(col_bc, pattern=[[0, P]], base=EXPERTS, channel_multiplier=1,
                           allow_small_or_imprecise_dtypes=True))
            for q in range(4):
                rows = slice(32 * q, 32 * q + 32)
                settle(pool)
                step(pool.memset(thr[rows, :], float(P * (q + 1))))
                settle(pool)
                step(pool.iota(mod32[rows, :], pattern=[[0, 1]], base=0, channel_multiplier=1,
                               allow_small_or_imprecise_dtypes=True))
                settle(pool)
                step(pool.iota(mod_bc[rows, :], pattern=[[0, P]], base=0, channel_multiplier=1,
                               allow_small_or_imprecise_dtypes=True))
            settle(pool)
            step(pool.iota(tab_f, pattern=[[0, 2], [1, BLOCKS]], base=0, channel_multiplier=0,
                           allow_small_or_imprecise_dtypes=True))
            settle(pool)
            pool.affine_select(out=tris, in_=tris, compare_op=ALU.is_ge, fill=0.0, base=-1, pattern=[[1, P]],
                               channel_multiplier=-1).then_inc(S["iota_ready"], 1)
            pool.wait_ge(S["b1_landed"], 48)
            pool.wait_ge(S["mt_turned"], KD)
            step(pool.tensor_copy(b1_parts[0:96, :], b1_raw[0:96, :]))
            settle(pool)
            for first in (32, 64):
                for r in range(first, 96, 32):
                    step(pool.tensor_tensor(b1_raw[r:r + 32, :], b1_raw[r:r + 32, :], b1_parts[r:r + 32, :],
                                            ALU.subtract))
                    settle(pool)
                for r in range(first, 96, 32):
                    step(pool.tensor_copy(b1_parts[r:r + 32, :], b1_raw[r:r + 32, :]))
                    settle(pool)
            pool.memset(xg, 0.0).then_inc(S["b1_ready"], 1)
            pool.wait_ge(S["b1_ready"], 1)
            pool.wait_ge(S["rows_stored"], 16 * TT)

            pool.wait_ge(S["tables_ready"], 1)
            n_more = pool.value_load(tab_n, min_val=EXPERTS - 3, max_val=MAX_BLOCKS - 3)

            def column(b):
                return pool.value_load(tab_col[:, bass.ds(b, 1) if not isinstance(b, int) else slice(b, b + 1)],
                                       min_val=0, max_val=P - 1)

            def gather(b, staged):
                col, limit = column(b), pool.to_reg(TOK - 1)
                at_least(pool, S["tx_done"], b)
                pool.tensor_copy(stage_g, slot_tok[:, bass.ds(col, 1)]).then_inc(S["stage"], 1)
                pool.wait_ge(S["stage"], staged)
                pool.sem_inc(S["dma_go"], 1)
                pool.indirect_dma_start(xg, None, rows_dram, bass.IndirectOffsetOnAxis(stage_g, 0),
                                        bounds_check=limit, oob_is_err=False).then_inc(S["xg_landed"], 16)

            def scatter(b, staged):
                col, limit = column(b), pool.to_reg(TOK - 1)
                at_least(pool, S["scattered"], b * 16)
                pool.tensor_copy(stage_s, slot_tok[:, bass.ds(col, 1)]).then_inc(S["stage"], 1)
                pool.wait_ge(S["stage"], staged)
                pool.wait_ge(S["ys_ready"], b + 1)
                pool.sem_inc(S["dma_go"], 1)
                pool.indirect_dma_start(moe_dram, bass.IndirectOffsetOnAxis(stage_s, 0), ys, None,
                                        bounds_check=limit, oob_is_err=False,
                                        compute_op=ALU.add).then_inc(S["scattered"], 16)

            for b in range(3):
                gather(b, b + 1)
            pool.wait_ge(S["moe_stored"], 16 * 2 * TT)
            with pool.Fori(0, n_more) as i:
                b = i + 2
                gather(b + 1, 2 * b)
                scatter(b - 2, 2 * b + 1)
            for last in range(3):
                scatter(n_more + last, 2 * n_more + (4 + last))

        @block.scalar
        def _(act):
            act.wait_ge(S["cols_ready"], 1)
            act.activation(c_sig, cols[:, C_C:C_C + 8], ACT.Sigmoid).then_inc(S["c_sig_ready"], 1)

            def root(sums, n, done, value):
                act.wait_ge(S[done], value)
                act.activation(sums, sums, ACT.Sqrt, bias=eps, scale=1.0 / n).then_inc(S["root_ready"], 1)

            act.wait_ge(S["x_landed"], 16)
            for t in range(TT):
                act.activation(xh[:, t], x_sb[:, t], ACT.Square, accum_out=ssq[:, t:t + 1]).then_inc(S["sq_ready"], 1)
            root(ssq, D, "sq_ready", TT)

            def row_copy(j):
                act.wait_ge(S["row_done"], j + 1)
                at_least(act, S["spread_done"], j)
                src = bank(j % 2 if j < 4 else 7)
                act.activation(row[:, :], src, ACT.Copy).then_inc(S["row_copied"], 1)

            for j in range(4):
                row_copy(j)
            act.wait_ge(S["lb_act"], 2)
            act.activation(lb0, lb0, ACT.Exp).then_inc(S["lb_act"], 1)
            act.activation(lb1, lb1, ACT.Exp).then_inc(S["lb_act"], 1)
            act.wait_ge(S["mod_done"], 5)
            for k in range(KD):
                act.wait_ge(S["xt_done"], k + 1)
                act.activation(ht[:, k, :], bank(2 + k % 4), ACT.Identity, bias=mod[:, k:k + 1],
                               scale=s1c[:, k:k + 1]).then_inc(S["ht_ready"], 1)

            def hg(i):
                if i == 1:
                    act.wait_ge(S["hg_dve"], 5)
                    act.activation(ks, fb[:, :], ACT.Ln).then_inc(S["hg_act"], 1)
                elif i == 3:
                    act.wait_ge(S["hg_dve"], 7)
                    act.activation(sr, fb[:, :], ACT.Exp).then_inc(S["hg_act"], 1)
                    act.activation(ks, klt, ACT.Exp).then_inc(S["hg_act"], 1)
                elif i == 5:
                    act.wait_ge(S["hg_dve"], 10)
                    act.activation(ks, klt, ACT.Exp, scale=-1.0).then_inc(S["hg_act"], 1)
                elif i == 7:
                    act.wait_ge(S["hg_dve"], 12)
                    act.activation(sr, klt, ACT.Exp).then_inc(S["hg_act"], 1)
                    act.activation(dec.rearrange("p (h c) -> p h c", h=HEADS),
                                   f3.rearrange("p h (c s) -> p h c s", s=CHUNK)[:, :, :, CHUNK - 1],
                                   ACT.Exp).then_inc(S["hg_act"], 1)

            for u, (kind, i, _, _) in enumerate(UNITS):
                src = bank(u % 3)
                if u in GATED:
                    n = GATED.index(u)
                    if kind == "x":
                        act.wait_ge(S["conv_ready"], i + 1)
                        src = conv_tmp[:, i % 2]
                    else:
                        act.wait_ge(S["proj_done"], u + 1)
                    if n >= 2:
                        act.wait_ge(S["evac_dve"], gated_done(n - 2))
                    act.activation(sig_tmp[:, n % 2], src, ACT.Sigmoid).then_inc(S["sig_ready"], 1)
                elif kind == "f":
                    act.wait_ge(S["proj_done"], u + 1)
                    act.activation(f3[:, i], src, ACT.Sigmoid).then_inc(S["evac_act"], 1)
                elif kind == "i":
                    act.wait_ge(S["proj_done"], u + 1)
                    act.activation(v3[:, i], src, ACT.Copy).then_inc(S["evac_act"], 1)
                if 7 <= u <= 15:
                    hg(u - 7)
            for t in range(TT):
                act.wait_ge(S["klt_turned"], t + 1)
                act.activation(klt3[:, t], bank(t % 3), ACT.Copy).then_inc(S["klt_ready"], 1)

            def o_square(t):
                act.wait_ge(S["o_done"], t + 1)
                for h in range(HEADS):
                    act.activation(sig_tmp[:, 0, h * P:(h + 1) * P], bank(t % 3)[:, h * P:(h + 1) * P], ACT.Square,
                                   accum_out=ssh[:, 4 * t + h:4 * t + h + 1]).then_inc(S["o_sq"], 1)
                root(ssh[:, 4 * t:4 * t + 4], P, "o_sq", 4 * t + 4)

            row_copy(4)
            o_square(0)
            row_copy(5)
            o_square(1)
            row_copy(6)
            o_square(2)
            o_square(3)
            row_copy(7)

            act.wait_ge(S["dt_dve"], 1)
            act.activation(dt_tmp, dt_tmp, ACT.Exp, scale=-1.0).then_inc(S["dt_act"], 1)
            act.activation(na, alog, ACT.Exp).then_inc(S["dt_act"], 1)
            act.wait_ge(S["dt_act"], 1)
            act.activation(dt_tmp, dt_tmp, ACT.Ln, bias=1.0).then_inc(S["dt_act"], 1)
            act.wait_ge(S["acum_ready"], 1)
            act.activation(ea, acum, ACT.Exp).then_inc(S["ea_ready"], 1)
            for t in range(TT):
                act.wait_ge(S["m_turned"], t + 1)
                act.activation(xs, bank(0), ACT.Copy).then_inc(S["m_copied"], 1)
                act.activation(btk, bank(1)[:, 0:256], ACT.Copy).then_inc(S["m_copied"], 1)
                act.wait_ge(S["m_seg"], t + 1)
                act.activation(seg, seg, ACT.Exp).then_inc(S["m_exp"], 1)
                act.activation(wgt, wgt, ACT.Exp).then_inc(S["m_exp"], 1)
                act.activation(eal, last, ACT.Exp).then_inc(S["m_exp"], 1)
                row_copy(8 + t)
                act.wait_ge(S["m_gated"], t + 1)
                for g in range(2):
                    act.activation(m_junk[:, g * 256:(g + 1) * 256], z3[:, t, g * 256:(g + 1) * 256], ACT.Square,
                                   accum_out=ssh[:, 2 * t + g:2 * t + g + 1]).then_inc(S["m_sq"], 1)
                root(ssh[:, 2 * t:2 * t + 2], 256, "m_sq", 2 * t + 2)
            for k in range(KD):
                act.wait_ge(S["mt_turned"], k + 1)
                w = cols[:, C_HGN:C_HGN + 1] if k < 4 else cols[:, C_SSMN + k - 4:C_SSMN + k - 3]
                act.activation(ht[:, k, :], bank(k % 4), ACT.Copy, scale=w).then_inc(S["mt_ready"], 1)
            for t in range(TT):
                act.wait_ge(S["x2_ready"], 5 + t)
                act.activation(xh[:, t], x_sb[:, t], ACT.Square, accum_out=ssq[:, t:t + 1]).then_inc(S["sq2_ready"], 1)
            root(ssq, D, "sq2_ready", TT)

            def high(n, slot, count, part):
                act.wait_ge(raw_landed[slot], 16 * count)
                at_least(act, S["w_used"], n - PARTS + 1)
                act.activation(w_hi[part][:, :], raw[slot][:, :], ACT.Copy).then_inc(S["hi_done"], 1)

            def high_first(n):
                high(n, n % RAW, n // RAW + 1, n % PARTS)

            act.wait_ge(S["win_used"], len(LOADS))
            for n in range(3):
                high_first(n)
            for k in range(KD):
                act.wait_ge(S["xt2_done"], k + 1)
                act.activation(ht[:, k, :], bank(k % 4), ACT.Identity, bias=mod[:, 24 + k:25 + k],
                               scale=s2c[:, k:k + 1]).then_inc(S["ht2_ready"], 1)

            high_first(3)

            def rows_out(t):
                act.wait_ge(S["rows_turned"], t + 1)
                act.activation(h2_rows[t], bank(5, 2), ACT.Copy).then_inc(S["rows_ready"], 1)

            rows_out(0)
            rows_out(1)
            act.wait_ge(S["route_act"], 1)
            act.activation(gate_e, gate_e, ACT.Exp).then_inc(S["route_act"], 1)
            rows_out(2)
            rows_out(3)

            def first_content(n):
                act.wait_ge(S["moe_init"], n + 1)
                if n == 4:
                    act.wait_ge(S["moe_stored"], 16 * 4)
                act.activation(ht[:, 4 + n % 4, :], bank(4 + n % 2), ACT.Copy).then_inc(S["fin_act"], 1)
                act.wait_ge(S["fin_act"], n + 1)
                t, h = n // 2, n % 2
                act.dma_start(moe_dram[t * P:(t + 1) * P, h * HALF:(h + 1) * HALF], ht[:, 4 + n % 4, :]).then_inc(
                    S["moe_stored"], 16)

            act.wait_ge(S["tables_ready"], 1)
            n_more = act.value_load(tab_n, min_val=EXPERTS - 3, max_val=MAX_BLOCKS - 3)

            def sigmoid(b):
                act.wait_ge(S["clipped"], 2 * b + 1)
                act.activation(sg, glu, ACT.Sigmoid, scale=ALPHA).then_inc(S["sig2_ready"], 1)

            def results(b, units):
                col = act.value_load(tab_col[:, bass.ds(b, 1)], min_val=0, max_val=P - 1)
                act.wait_ge(S["w_used"], units)
                at_least(act, S["scattered"], b * 16)
                act.activation(ys, bank(4, 2), ACT.Copy, scale=slot_gate[:, bass.ds(col, 1)]).then_inc(S["ys_ready"], 1)

            def turned(b):
                act.wait_ge(S["ta_done"], b + 1)
                act.activation(flat(a_hi[:, :, :]), bank(6, 2), ACT.Copy).then_inc(S["a_hi_ready"], 1)

            def x_high(b, units):
                act.wait_ge(S["tx_done"], b + 1)
                at_least(act, S["w_used"], units)
                act.activation(flat(x_hi[:, :, :]), bank(6, 2), ACT.Copy).then_inc(S["x_hi_ready"], 1)

            def high_in_turn(i, j):
                high(unit(i, j), (2 * UNITS_W1 + j) % RAW, landings(i, j), j % PARTS)

            x_high(0, 0)
            for n in range(4, UNITS_W1):
                high_first(n)
                first_content(n - 4)
            high_first(8)
            for n in (4, 5, 6, 7):
                first_content(n)
            x_high(1, UNITS_W1)
            high_first(9)
            sigmoid(0)
            for n in range(10, 15):
                high_first(n)
            turned(0)
            high_first(15)

            def turn(i):
                b = i + 2
                for j in range(3):
                    high_in_turn(i, j)
                x_high(b, unit(i, 0))
                high_in_turn(i, 3)
                sigmoid(b - 1)
                for j in range(4, 8):
                    high_in_turn(i, j)
                results(b - 2, unit(i, UNITS_W2))
                for j in range(8, 11):
                    high_in_turn(i, j)
                turned(b - 1)
                high_in_turn(i, 11)

            with act.Fori(0, n_more) as i:
                turn(i)
            turn(n_more)
            high_in_turn(n_more + 1, 0)
            sigmoid(n_more + 2)
            for j in range(1, 5):
                high_in_turn(n_more + 1, j)
            results(n_more + 1, unit(n_more + 1, UNITS_W2))
            turned(n_more + 2)
            for j in range(5, 8):
                high_in_turn(n_more + 1, j)
            results(n_more + 2, unit(n_more + 1, 2 * UNITS_W2))
            for t in range(TT):
                act.wait_ge(S["fin"], t + 1)
                act.activation(xh[:, t], x_sb[:, t], ACT.Square, accum_out=ssq[:, t:t + 1]).then_inc(S["fin_act"], 1)
                root(ssq[:, t:t + 1], D, "fin_act", 2 * TT + t + 1)

        @block.tensor
        def _(pe):
            mm = pe.matmul
            pe.wait_ge(S["small_landed"], 16 * 9)
            pe.wait_ge(S["consts_ready"], 1)
            pe.transpose(bank(6)[:, 0:SMALL_ROWS], small_rows, ident[0:SMALL_ROWS, 0:SMALL_ROWS]).then_inc(
                S["cols_turned"], 1)

            def landed(n):
                pe.wait_ge(win_landed[n % 2], 16 * (n // 2 + 1))

            def ada_row(j):
                n = j if j < 4 else L_ADA2 + j - 4
                b = j % 2 if j < 4 else 7
                if j == 0:
                    pe.wait_ge(S["c_ready"], 1)
                elif 2 <= j < 4:
                    pe.wait_ge(S["row_copied"], j - 1)
                elif j > 4:
                    pe.wait_ge(S["mod_done"], j + 1)
                landed(n)
                for k in range(KD):
                    g = 32 * (k % 4)
                    ins = mm(bank(b)[g:g + 32, :], c_pad[:, k, :], win[:, n % 2, k, :], start=(k < 4),
                             stop=(k >= 4), skip_group_check=True)
                ins.then_inc(S["row_done"], 1)

            def ada_spread(j):
                pe.wait_ge(S["row_copied"], j + 1)
                dst = bank(2 + j if j < 4 else 7)
                if j in (4, 5, 10, 11):
                    ins = mm(dst, ones[:, :], row[:, :], start=True, stop=True)
                else:
                    for i in range(4):
                        ins = mm(dst[:, i:i + 1], row[:, i * P:(i + 1) * P], ones[:, 0:1], start=True, stop=True)
                ins.then_inc(S["spread_done"], 1)

            def release(done, value):
                pe.wait_ge(S[done], value)
                pe.sem_inc(S["win_used"], 1)

            for j in range(4):
                ada_row(j)
                if j >= 1:
                    ada_spread(j - 1)
                release("row_done", j + 1)
            ada_spread(3)
            pe.wait_ge(S["xh_ready"], TT)
            pe.wait_ge(S["mod_done"], 5)
            for k in range(KD):
                if k >= 4:
                    pe.wait_ge(S["ht_ready"], k - 3)
                for t in range(TT):
                    ins = pe.transpose(bank(2 + k % 4)[:, t * P:(t + 1) * P], xh[:, t, k * P:(k + 1) * P], ident[:, :])
                ins.then_inc(S["xt_done"], 1)
            pe.wait_ge(S["ht_ready"], KD)

            for u, (kind, i, n, _) in enumerate(UNITS):
                if u >= 3:
                    who, count = evacuated(u - 3)
                    pe.wait_ge(S["evac_" + who], count)
                b = bank(u % 3)
                if kind == "dt":
                    pe.wait_ge(S["dt_w_landed"], 16)
                    for t in range(TT):
                        for k in range(KD):
                            ins = mm(b[:, 8 * t:8 * t + 8], ht[:, k, t * P:(t + 1) * P], wdt[:, k, :],
                                     start=(k == 0), stop=(k == KD - 1))
                    ins.then_inc(S["proj_done"], 1)
                    continue
                landed(n)
                w = win[:, n % 2]
                j = i % 4
                for k in range(KD):
                    if kind in "qfx":
                        ins = mm(b, w[:, k, j * P:(j + 1) * P], ht[:, k, :], start=(k == 0), stop=(k == KD - 1))
                    else:
                        ins = mm(b, ht[:, k, i * P:(i + 1) * P], w[:, k, :], start=(k == 0), stop=(k == KD - 1))
                ins.then_inc(S["proj_done"], 1)
                if j == 3:
                    release("proj_done", u + 1)

            pe.wait_ge(S["hg_dve"], 14)
            for t in range(TT):
                for h in range(HEADS):
                    for j, a, b in QUARTERS:
                        ins = mm(bank(3 + t)[32 * j:32 * j + 32, h * P + a:h * P + b],
                                 ks3[:, h, t * P + 32 * j:t * P + 32 * j + 32], q3[:, h, t * P + a:t * P + b],
                                 start=True, stop=True, skip_group_check=True)
                ins.then_inc(S["att_done"], 1)
            pe.wait_ge(S["evac_dve"], evacuated(len(UNITS) - 1)[1])
            pe.wait_ge(S["evac_act"], 8)
            for t in range(TT):
                if t == 3:
                    pe.wait_ge(S["klt_ready"], 1)
                for h in range(HEADS):
                    ins = pe.transpose(bank(t % 3)[:, h * P:(h + 1) * P], k3[:, h, t * P:(t + 1) * P], ident[:, :])
                ins.then_inc(S["klt_turned"], 1)

            def ada_filler_row(j):
                ada_row(j)
                release("row_done", j + 1)

            def state(ch):
                if ch == 0:
                    pe.wait_ge(S["att_masked"], 4 * TT)
                    pe.wait_ge(S["vp_ready"], 2)
                if ch >= 4:
                    pe.wait_ge(S["s_ready"], ch - 3)
                pe.wait_ge(S["klt_ready"], ch // 2 + 1)
                for h in range(HEADS):
                    hs = slice(h * P, (h + 1) * P)
                    ins = mm(bank(3 + ch % 4)[:, hs], klt3[:, ch // 2, hs], vp[:, ch, hs], start=True, stop=True)
                ins.then_inc(S["ds_done"], 1)

            def output(t):
                if t == 0:
                    pe.wait_ge(S["klt_ready"], TT)
                if t == 3:
                    pe.wait_ge(S["o_normed"], 1)
                pe.wait_ge(S["s_ready"], 2 * t + 1)
                for h in range(HEADS):
                    hs = slice(h * P, (h + 1) * P)
                    dst = bank(t % 3)[:, hs]
                    mm(dst, att3[:, t, hs], v3[:, t, hs], start=True, stop=False)
                    if t > 0:
                        mm(dst, qep[:, h, 2 * t, :], sr3[:, (2 * t) % 4, hs], start=False, stop=False)
                    ins = mm(dst, qep[:, h, 2 * t + 1, :], sr3[:, (2 * t + 1) % 4, hs], start=False, stop=True)
                ins.then_inc(S["o_done"], 1)

            ada_filler_row(4)
            state(0)
            state(1)
            state(2)
            ada_spread(4)
            output(0)
            state(3)
            state(4)
            ada_filler_row(5)
            ada_spread(5)
            output(1)
            state(5)
            state(6)
            ada_filler_row(6)
            ada_spread(6)
            output(2)
            output(3)
            ada_filler_row(7)
            ada_spread(7)

            pe.wait_ge(S["dt_dve"], 3)
            pe.wait_ge(S["s_ready"], 7)
            mm(bank(6)[:, 0:32], tri[:, :], dta, start=True, stop=True).then_inc(S["acum_done"], 1)
            pe.wait_ge(S["o_normed"], TT)
            for t in range(TT):
                ts = slice(t * P, (t + 1) * P)
                at_least(pe, S["m_free"], t)
                for i in range(4):
                    pe.transpose(bank(0)[:, i * P:(i + 1) * P], xbc[:, i, ts], ident[:, :])
                for g in range(2):
                    pe.transpose(bank(1)[:, g * P:(g + 1) * P], xbc[:, 4 + g, ts], ident[:, :])
                for g in range(2):
                    ins = mm(bank(1)[:, 256 + g * P:256 + (g + 1) * P], xbc[:, 4 + g, ts], xbc[:, 6 + g, ts],
                             start=True, stop=True)
                ins.then_inc(S["m_turned"], 1)
                pe.wait_ge(S["dtri_ready"], t + 1)
                for i in range(2):
                    ins = mm(bank(2 + i), ones[:, :], dtri[:, 4 * i:4 * i + 4, :], start=True, stop=True)
                ins.then_inc(S["acb_done"], 1)
                ada_filler_row(8 + t)
                ada_spread(8 + t)
                pe.wait_ge(S["m_ready"], t + 1)
                for h in range(SSM_HEADS):
                    mm(bank(4)[:, h * 64:(h + 1) * 64], seg[:, h, :], xdt[:, h * 64:(h + 1) * 64], start=True, stop=True)
                if t > 0:
                    for g in range(2):
                        mm(bank(5)[:, g * 256:(g + 1) * 256], xbc[:, 6 + g, ts], sm[:, g * 256:(g + 1) * 256],
                           start=True, stop=True)
                for g in range(2):
                    ins = mm(bank(6)[:, g * 256:(g + 1) * 256], btk[:, g * P:(g + 1) * P],
                             xw[:, g * 256:(g + 1) * 256], start=True, stop=True)
                ins.then_inc(S["my_done"], 1)

            pe.wait_ge(S["y_ready"], TT)
            for k in range(KD):
                if k >= 4:
                    pe.wait_ge(S["mt_ready"], k - 3)
                src = g3 if k < 4 else z3
                for t in range(TT):
                    ins = pe.transpose(bank(k % 4)[:, t * P:(t + 1) * P], src[:, t, (k % 4) * P:(k % 4 + 1) * P],
                                       ident[:, :])
                ins.then_inc(S["mt_turned"], 1)
            pe.wait_ge(S["mt_ready"], KD)
            pe.wait_ge(S["mod_done"], 13)
            for h in range(2):
                landed(L_OUT + h)
                for t in range(TT):
                    u = 4 * h + t
                    at_least(pe, S["x2_ready"], u - 3)
                    for k in range(KD):
                        ins = mm(bank(4 + u % 4), ht[:, k, t * P:(t + 1) * P], win[:, (L_OUT + h) % 2, k, :],
                                 start=(k == 0), stop=(k == KD - 1))
                    ins.then_inc(S["mix_done"], 1)
                release("mix_done", 4 * h + 4)

            pe.wait_ge(S["xh2_ready"], TT)
            for k in range(KD):
                if k >= 4:
                    pe.wait_ge(S["ht2_ready"], k - 3)
                for t in range(TT):
                    ins = pe.transpose(bank(k % 4)[:, t * P:(t + 1) * P], xh[:, t, k * P:(k + 1) * P], ident[:, :])
                ins.then_inc(S["xt2_done"], 1)
            pe.wait_ge(S["ht2_ready"], KD)
            pe.wait_ge(S["rw_landed"], 16)
            for t in range(TT):
                for k in range(KD):
                    ins = mm(bank(4)[:, t * 32:(t + 1) * 32], ht[:, k, t * P:(t + 1) * P], rw[:, k, :],
                             start=(k == 0), stop=(k == KD - 1))
            ins.then_inc(S["logits_done"], 1)

            def rows_back(t):
                at_least(pe, S["rows_ready"], t)
                for k in range(KD):
                    ins = pe.transpose(bank(5, 2)[:, k * P:(k + 1) * P], ht[:, k, t * P:(t + 1) * P], ident[:, :])
                ins.then_inc(S["rows_turned"], 1)

            rows_back(0)
            rows_back(1)

            pe.wait_ge(S["route_pe"], 1)
            pe.wait_ge(S["iota_ready"], 1)
            for t in range(TT):
                for s in range(t):
                    mm(bank(0)[:, t * 32:(t + 1) * 32], ones[:, :], member[:, s, :], start=(s == 0), stop=False)
                ins = mm(bank(0)[:, t * 32:(t + 1) * 32], tris, member[:, t, :], start=(t == 0), stop=True)
            ins.then_inc(S["route"], 1)
            pe.wait_ge(S["route_pe"], 2)
            for t in range(TT):
                ins = mm(bank(1)[0:96, 0:1], member3[:, t, :, :].rearrange("p r e -> p (r e)"), ones[:, 0:1],
                         start=(t == 0), stop=(t == TT - 1))
            ins.then_inc(S["route"], 1)
            pe.wait_ge(S["route_pe"], 3)
            mm(bank(2)[0:96, 0:1], tris[0:96, 0:96], more[0:96, :], start=True, stop=True)
            mm(bank(2)[:, 1:2], ones[0:96, :], more[0:96, :], start=True, stop=True).then_inc(S["route"], 1)
            pe.wait_ge(S["route_pe"], 4)
            mm(bank(3)[:, 0:EXTRA], mod_bc[0:96, :], ext_hot[0:96, :], start=True, stop=True)
            mm(bank(3)[:, EXTRA:2 * EXTRA], col_bc[0:96, :], ext_hot[0:96, :], start=True, stop=True).then_inc(S["route"], 1)
            rows_back(2)
            rows_back(3)
            pe.wait_ge(S["route_pe"], 5)
            for t in range(TT):
                ins = pe.transpose(bank(7)[0:EXPERTS, t * P:(t + 1) * P], gate_dense[:, t, :], ident[:, :])
            ins.then_inc(S["route"], 1)
            for n in range(TT * TOP):
                pe.wait_ge(S["route_pe"], 7 + n)
                ins = mm(bank(4)[:, 0:256], lo_hot[:, n % 2, :], key_hot[:, n % 2, :], start=(n == 0),
                         stop=(n == TT * TOP - 1))
                ins.then_inc(S["route"], 1)
            pe.wait_ge(S["b2_landed"], 16)
            pe.wait_ge(S["tables_ready"], 1)
            pe.wait_ge(S["rows_ready"], TT)

            def moe_first(n):
                at_least(pe, S["fin_act"], n - 1)
                t, h = n // 2, n % 2
                mm(bank(4 + n % 2), gates_t[:, t * P:(t + 1) * P], b2_sb[:, h * HALF:(h + 1) * HALF],
                   start=True, stop=True).then_inc(S["moe_init"], 1)

            pe.wait_ge(S["b1_ready"], 1)
            n_more = pe.value_load(tab_n, min_val=EXPERTS - 3, max_val=MAX_BLOCKS - 3)

            def turn_x(b):
                pe.wait_ge(S["xg_landed"], 16 * b + 16)
                at_least(pe, S["xgt_ready"], b)
                at_least(pe, S["actt_ready"], b - 1)
                for k in range(KD):
                    ins = pe.transpose(bank(6, 2)[:, k * P:(k + 1) * P], xg[:, k * P:(k + 1) * P], ident[:, :])
                ins.then_inc(S["tx_done"], 1)

            def three(dst, a, hi, lo, at, first, last):
                cs = slice(at, at + HALF)
                mm(dst, a[0], hi[:, cs], start=first, stop=False)
                mm(dst, a[0], lo[:, cs], start=False, stop=False)
                return mm(dst, a[1], hi[:, cs], start=False, stop=last)

            def hidden(b, unit_of, after):
                pe.wait_ge(S["xgt_ready"], b + 1)
                pe.wait_ge(S["sel_ready"], b + 1)
                at_least(pe, S["clipped"], 2 * b)
                for n in range(4):
                    mm(bank(n), sel[0:96, :], b1_parts[0:96, n * HALF:(n + 1) * HALF], start=True, stop=False)
                for k in range(KD):
                    number, part = unit_of(k)
                    pe.wait_ge(S["lo_done"], number + 1)
                    for n in range(4):
                        ins = three(bank(n), (x_hi[:, k, :], x_lo[:, k, :]), w_hi[part], w_lo[part], n * HALF,
                                    False, k == KD - 1)
                    ins.then_inc(S["w_used"], 1)
                    if k in after:
                        after[k]()
                    if isinstance(b, int) and b == 0:
                        moe_first(k)

            def turn_act(b, xs_turned):
                pe.wait_ge(S["act_ready"], b + 1)
                pe.wait_ge(S["xgt_ready"], xs_turned)
                for k in range(KD):
                    ins = pe.transpose(bank(6, 2)[:, k * P:(k + 1) * P], act_sb[:, k * P:(k + 1) * P], ident[:, :])
                ins.then_inc(S["ta_done"], 1)

            def results(b, unit_of):
                pe.wait_ge(S["actt_ready"], b + 1)
                pe.wait_ge(S["fin_act"], 2 * TT)
                at_least(pe, S["ys_ready"], b)
                for u in range(UNITS_W2):
                    number, part = unit_of(u)
                    pe.wait_ge(S["lo_done"], number + 1)
                    for k in (2 * u, 2 * u + 1):
                        for n in range(2):
                            ins = three(bank(4 + n), (a_hi[:, k, :], a_lo[:, k, :]), w_hi[part], w_lo[part],
                                        (k % 2) * D + n * HALF, k == 0, k == KD - 1)
                    ins.then_inc(S["w_used"], 1)

            ACT_AFTER, X_AFTER = 3, 7
            turn_x(0)
            hidden(0, lambda k: (k, k % PARTS), {3: lambda: turn_x(1)})
            hidden(1, lambda k: (UNITS_W1 + k, k % PARTS),
                   {ACT_AFTER: lambda: turn_act(0, 2), X_AFTER: lambda: turn_x(2)})

            def turn(i, more):
                b = i + 2
                results(b - 2, lambda u: (unit(i, u), u % PARTS))
                after = {ACT_AFTER: lambda: turn_act(b - 1, b + 1)}
                if more:
                    after[X_AFTER] = lambda: turn_x(b + 1)
                hidden(b, lambda k: (unit(i, UNITS_W2 + k), k % PARTS), after)

            with pe.Fori(0, n_more) as i:
                turn(i, True)
            turn(n_more, False)
            results(n_more + 1, lambda u: (unit(n_more + 1, u), u % PARTS))
            turn_act(n_more + 2, n_more + 3)
            results(n_more + 2, lambda u: (unit(n_more + 1, UNITS_W2 + u), u % PARTS))

        @block.vector
        def _(dve):
            step, settle = order("dve_order")
            V = nc.vector
            dve.wait_ge(S["cols_turned"], 1)
            V.tensor_copy(cols[:, 0:SMALL_ROWS], bank(6)[:, 0:SMALL_ROWS]).then_inc(S["cols_ready"], 1)
            dve.wait_ge(S["c_sig_ready"], 1)
            dve.wait_ge(S["consts_ready"], 1)
            V.tensor_tensor(c_pad[:, :, 0], cols[:, C_C:C_C + 8], c_sig, ALU.mult).then_inc(S["c_ready"], 1)
            row0, row1 = cols[:, C_LB:C_LB + 4], cols[:, C_LB + 4:C_LB + 8]
            step(V.tensor_tensor(oml, row0, row1, ALU.max))
            settle(dve)
            V.tensor_tensor(lb0, row0, oml, ALU.subtract).then_inc(S["lb_act"], 1)
            V.tensor_tensor(lb1, row1, oml, ALU.subtract).then_inc(S["lb_act"], 1)

            def rms_factor(dst, root, n):
                dve.wait_ge(S["root_ready"], n)
                step(V.reciprocal(dst, root))
                settle(dve)

            rms_factor(rstd, ssq, 1)
            for t in range(TT):
                V.tensor_scalar(xh[:, t], x_sb[:, t], rstd[:, t:t + 1], None, ALU.mult).then_inc(S["xh_ready"], 1)

            def ada_add(j):
                dve.wait_ge(S["spread_done"], j + 1)
                src = bank(2 + j if j < 4 else 7)
                if j in (4, 5, 10, 11):
                    dst = (g1_b if j < 6 else g2_b)[:, (j % 2) * HALF:(j % 2 + 1) * HALF]
                    dve.wait_ge(S["gate_bias_landed"], 32)
                    V.tensor_tensor(dst, src, dst, ALU.add).then_inc(S["mod_done"], 1)
                else:
                    V.tensor_tensor(mod[:, 4 * j:4 * j + 4], src[:, 0:4], cols[:, 4 * j:4 * j + 4], ALU.add).then_inc(
                        S["mod_done"], 1)

            for j in range(4):
                ada_add(j)
            dve.wait_ge(S["mod_done"], 4)
            V.scalar_tensor_tensor(out=s1c, in0=mod[:, 8:16], scalar=1.0, in1=cols[:, C_N1:C_N1 + 8], op0=ALU.add,
                                   op1=ALU.mult).then_inc(S["mod_done"], 1)
            dve.wait_ge(S["lb_act"], 4)
            step(V.tensor_tensor(lbs, lb0, lb1, ALU.add))
            settle(dve)
            step(V.reciprocal(lbs, lbs))
            settle(dve)
            step(V.tensor_tensor(lb0, lb0, lbs, ALU.mult))
            settle(dve)
            step(V.tensor_scalar(oml, lb0, -1.0, 1.0, ALU.mult, ALU.add))
            settle(dve)

            chunked = lambda a: a.rearrange("p (c s) -> p c s", s=CHUNK)

            def at_chunk(i):
                return chunked(fb[:, :])[:, :, i:i + 1].to_broadcast([P, HEADS * CHUNKS, CHUNK])

            def hg(i):
                done = S["hg_dve"]
                if i == 0:
                    dve.wait_ge(S["evac_act"], 4)
                    for h in range(HEADS):
                        V.tensor_scalar(f3[:, h], f3[:, h], oml[:, h:h + 1], lb0[:, h:h + 1], ALU.mult,
                                        ALU.add).then_inc(done, 1)
                    dve.wait_ge(done, 4)
                    V.tensor_scalar(kb[:, :], fb[:, :], -1.0, 1.0, ALU.mult, ALU.add).then_inc(done, 1)
                elif i == 2:
                    dve.wait_ge(S["hg_act"], 1)
                    V.tensor_tensor_scan(fb[:, :], scan_mask[:, :], ks, 0.0, ALU.mult, ALU.add).then_inc(done, 1)
                    dve.wait_ge(done, 6)
                    V.tensor_tensor(chunked(klt), chunked(fb[:, :]), at_chunk(CHUNK // 2 - 1),
                                    ALU.subtract).then_inc(done, 1)
                elif i == 4:
                    dve.wait_ge(S["hg_act"], 2)
                    dve.wait_ge(S["pads_ready"], 1)
                    dve.wait_ge(S["evac_dve"], 4)
                    qep5 = w1_flat[:, 2048:6144].rearrange("p (n a b s) -> p n a b s", a=2, b=2, s=CHUNK)
                    q4 = qb[:, :].rearrange("p (n a s) -> p n a s", a=2, s=CHUNK)
                    e4 = sr.rearrange("p (n a s) -> p n a s", a=2, s=CHUNK)
                    for a in range(2):
                        V.tensor_tensor(qep5[:, :, a, a, :], q4[:, :, a, :], e4[:, :, a, :], ALU.mult).then_inc(done, 1)
                    dve.wait_ge(S["hg_act"], 3)
                    dve.wait_ge(done, 9)
                    V.tensor_tensor(qb[:, :], qb[:, :], ks, ALU.mult).then_inc(done, 1)
                elif i == 6:
                    dve.wait_ge(S["hg_act"], 4)
                    V.tensor_tensor(ks, kb[:, :], ks, ALU.mult).then_inc(done, 1)
                    V.tensor_tensor(chunked(klt), at_chunk(CHUNK - 1), chunked(fb[:, :]), ALU.subtract).then_inc(done, 1)
                elif i == 8:
                    dve.wait_ge(S["hg_act"], 6)
                    V.tensor_tensor(kb[:, :], kb[:, :], sr, ALU.mult).then_inc(done, 1)
                    V.memset(fb[:, :], 0.0).then_inc(done, 1)

            for u, (kind, i, _, _) in enumerate(UNITS):
                src = bank(u % 3)
                freed = S["evac_dve"]
                if kind == "x":
                    dve.wait_ge(S["proj_done"], u + 1)
                    a = conv_tmp[:, i % 2]
                    w = lambda j: cols[:, C_CW + 8 * j + i:C_CW + 8 * j + i + 1]
                    step(V.tensor_scalar(a, src, w(CONV - 1), cols[:, C_CB + i:C_CB + i + 1], ALU.mult, ALU.add))
                    for d in range(1, CONV):
                        settle(dve)
                        ins = V.scalar_tensor_tensor(out=a[:, d:], in0=src[:, 0:TOK - d], scalar=w(CONV - 1 - d),
                                                     in1=a[:, d:], op0=ALU.mult, op1=ALU.add)
                        if d < CONV - 1:
                            step(ins)
                    ins.then_inc(S["conv_ready"], 1)
                    dve.wait_ge(S["sig_ready"], GATED.index(u) + 1)
                    V.tensor_tensor(xbc[:, i], a, sig_tmp[:, GATED.index(u) % 2], ALU.mult).then_inc(freed, 1)
                elif u in GATED:
                    if u == GATED[-4]:
                        dve.wait_ge(S["hg_dve"], 6)
                    dve.wait_ge(S["sig_ready"], GATED.index(u) + 1)
                    dst = {"q": q3, "g": g3, "z": z3}[kind][:, i]
                    V.tensor_tensor(dst, src, sig_tmp[:, GATED.index(u) % 2], ALU.mult).then_inc(freed, 1)
                elif kind == "dt":
                    dve.wait_ge(S["proj_done"], u + 1)
                    dve.wait_ge(S["bias_landed"], 64)
                    V.tensor_tensor(dtr.rearrange("p (t h) -> p t h", t=TT), src[:, 0:32].rearrange(
                        "p (t h) -> p t h", t=TT), dtb.unsqueeze(1).to_broadcast([P, TT, 8]), ALU.add).then_inc(freed, 1)
                if 7 <= u <= 15:
                    hg(u - 7)
            mask = block_mask[:, :].bitcast(I32)
            for t in range(TT):
                dve.wait_ge(S["att_done"], t + 1)
                for j, a, b in QUARTERS:
                    part = slice(32 * j, 32 * j + 32)
                    V.copy_predicated(att3[part, t].rearrange("p (h s) -> p h s", h=HEADS)[:, :, a:b],
                                      mask[part, a:b].unsqueeze(1).to_broadcast([32, HEADS, b - a]),
                                      bank(3 + t)[part].rearrange("p (h s) -> p h s", h=HEADS)[:, :, a:b]).then_inc(
                        S["att_masked"], 1)

            def state(ch):
                dve.wait_ge(S["ds_done"], ch + 1)
                new, old = sr3[:, (ch + 1) % 4], sr3[:, ch % 4]
                if ch == 0:
                    V.tensor_copy(new, bank(3)).then_inc(S["s_ready"], 1)
                    return
                dve.wait_ge(S["s_ready"], ch)
                if ch >= 3:
                    dve.wait_ge(S["o_done"], (ch - 3) // 2 + 1)
                for h in range(HEADS):
                    hs = slice(h * P, (h + 1) * P)
                    ins = V.scalar_tensor_tensor(out=new[:, hs], in0=old[:, hs], scalar=dec[:, 8 * h + ch:8 * h + ch + 1],
                                                 in1=bank(3 + ch % 4)[:, hs], op0=ALU.mult, op1=ALU.add)
                    if h < HEADS - 1:
                        step(ins)
                ins.then_inc(S["s_ready"], 1)

            def o_norm(t):
                rms_factor(rh[:, 4 * t:4 * t + 4], ssh[:, 4 * t:4 * t + 4], 2 + t)
                for h in range(HEADS):
                    hs = slice(h * P, (h + 1) * P)
                    ins = V.scalar_tensor_tensor(out=g3[:, t, hs], in0=bank(t % 3)[:, hs],
                                                 scalar=rh[:, 4 * t + h:4 * t + h + 1], in1=g3[:, t, hs],
                                                 op0=ALU.mult, op1=ALU.mult)
                    if h < HEADS - 1:
                        step(ins)
                ins.then_inc(S["o_normed"], 1)

            state(0)
            state(1)
            state(2)
            ada_add(4)
            o_norm(0)
            state(3)
            state(4)
            ada_add(5)
            o_norm(1)
            state(5)
            state(6)
            ada_add(6)
            o_norm(2)
            o_norm(3)
            ada_add(7)

            V.scalar_tensor_tensor(out=dt_tmp, in0=dtr, scalar=-1.0, in1=dtr, op0=ALU.mult,
                                   op1=ALU.max).then_inc(S["dt_dve"], 1)
            dve.wait_ge(S["dt_act"], 3)
            step(V.scalar_tensor_tensor(out=dtv, in0=dtr, scalar=0.0, in1=dt_tmp, op0=ALU.max, op1=ALU.add))
            V.tensor_scalar(na, na, -1.0, None, ALU.mult).then_inc(S["dt_dve"], 1)
            settle(dve)
            dve.wait_ge(S["dt_dve"], 2)
            over_t = lambda a: a.rearrange("p (t h) -> p t h", t=TT)
            V.tensor_tensor(over_t(dta), over_t(dtv), na.unsqueeze(1).to_broadcast([P, TT, 8]),
                            ALU.mult).then_inc(S["dt_dve"], 1)
            dve.wait_ge(S["dt_dve"], 3)
            dve.wait_ge(S["acum_done"], 1)
            V.tensor_copy(acum, bank(6)[:, 0:32]).then_inc(S["acum_ready"], 1)
            dve.wait_ge(S["acum_ready"], 1)
            heads = lambda a: a.rearrange("p (h s) -> p h s", h=SSM_HEADS)
            wide = lambda a: a.unsqueeze(2).to_broadcast([P, SSM_HEADS, 64])
            dve.wait_ge(S["o_done"], TT)
            for t in range(TT):
                h8 = slice(8 * t, 8 * t + 8)
                for h in range(SSM_HEADS):
                    ins = V.tensor_scalar(dtri[:, h, :], tri[:, :], dta[:, 8 * t + h:8 * t + h + 1], None, ALU.mult)
                    if h < SSM_HEADS - 1:
                        step(ins)
                ins.then_inc(S["dtri_ready"], 1)
                dve.wait_ge(S["m_copied"], 2 * t + 2)
                step(V.tensor_tensor(heads(xdt), heads(xs), wide(dtv[:, h8]), ALU.mult))
                step(V.tensor_tensor(cbm, bank(1)[:, 256:512].rearrange("p (g t) -> p g t", g=2),
                                     tri[:, :].unsqueeze(1).to_broadcast([P, 2, P]), ALU.mult))
                dve.wait_ge(S["acb_done"], t + 1)
                acb = bank(2, 2).rearrange("p (h t) -> p h t", h=SSM_HEADS)
                for h in range(SSM_HEADS):
                    step(V.tensor_scalar(seg[:, h, :], acb[:, h, :], acum[:, 8 * t + h:8 * t + h + 1], 0.0,
                                         ALU.subtract, ALU.min))
                step(V.tensor_copy(last, acb[:, :, P - 1]))
                settle(dve)
                V.tensor_tensor(wgt, last, acum[:, h8], ALU.subtract).then_inc(S["m_seg"], 1)
                dve.wait_ge(S["m_exp"], 3 * t + 3)
                for g in range(2):
                    step(V.tensor_tensor(seg[:, 4 * g:4 * g + 4, :], seg[:, 4 * g:4 * g + 4, :],
                                         cbm[:, g:g + 1, :].to_broadcast([P, 4, P]), ALU.mult))
                settle(dve)
                V.tensor_tensor(heads(xw), heads(xdt), wide(wgt), ALU.mult).then_inc(S["m_ready"], 1)
                ada_add(8 + t)
                step(V.tensor_tensor(heads(yt), heads(xs), wide(skip), ALU.mult))
                settle(dve)
                dve.wait_ge(S["my_done"], t + 1)
                step(V.tensor_tensor(yt, yt, bank(4), ALU.add))
                if t == 0:
                    step(V.tensor_copy(sm, bank(6)))
                    settle(dve)
                else:
                    dve.wait_ge(S["ea_ready"], 1)
                    step(V.tensor_tensor(heads(m_tmp), heads(bank(5)), wide(ea[:, h8]), ALU.mult))
                    step(V.tensor_tensor(heads(sm), heads(sm), wide(eal), ALU.mult))
                    settle(dve)
                    step(V.tensor_tensor(yt, yt, m_tmp, ALU.add))
                    step(V.tensor_tensor(sm, sm, bank(6), ALU.add))
                    settle(dve)
                V.tensor_tensor(z3[:, t], z3[:, t], yt, ALU.mult).then_inc(S["m_gated"], 1)
                rms_factor(rh[:, 2 * t:2 * t + 2], ssh[:, 2 * t:2 * t + 2], 6 + t)
                step(V.tensor_scalar(z3[:, t, 0:256], z3[:, t, 0:256], rh[:, 2 * t:2 * t + 1], None, ALU.mult))
                settle(dve)
                V.tensor_scalar(z3[:, t, 256:512], z3[:, t, 256:512], rh[:, 2 * t + 1:2 * t + 2], None,
                                ALU.mult).then_inc(S["y_ready"], 1)
                dve.wait_ge(S["y_ready"], t + 1)
                V.tensor_copy(m_tmp[:, 0:8], acum[:, 0:8]).then_inc(S["m_free"], 1)
            step(V.scalar_tensor_tensor(out=s2c, in0=mod[:, 32:40], scalar=1.0, in1=cols[:, C_N2:C_N2 + 8],
                                        op0=ALU.add, op1=ALU.mult))
            settle(dve)
            for u in range(2 * TT):
                h, t = u // TT, u % TT
                hs = slice(h * HALF, (h + 1) * HALF)
                dve.wait_ge(S["mix_done"], u + 1)
                tmp = (m_tmp, m_junk)[u % 2]
                at_least(dve, S["x2_ready"], u - 1)
                step(V.tensor_tensor(tmp, bank(4 + u % 4), g1_b[:, hs], ALU.mult))
                settle(dve)
                V.tensor_tensor(x_sb[:, t, hs], x_sb[:, t, hs], tmp, ALU.add).then_inc(S["x2_ready"], 1)
            rms_factor(rstd, ssq, 10)
            for t in range(TT):
                V.tensor_scalar(xh[:, t], x_sb[:, t], rstd[:, t:t + 1], None, ALU.mult).then_inc(S["xh2_ready"], 1)

            def low(n, slot, part):
                dve.wait_ge(S["hi_done"], n + 1)
                V.tensor_tensor(w_lo[part][:, :], raw[slot][:, :], w_hi[part][:, :].bitcast(F32),
                                ALU.subtract).then_inc(S["lo_done"], 1)

            def low_first(n):
                low(n, n % RAW, n % PARTS)

            for n in range(3):
                low_first(n)

            dve.wait_ge(S["logits_done"], 1)
            dve.wait_ge(S["iota_ready"], 1)
            step(V.tensor_tensor(logits, bank(4)[:, 0:128].rearrange("p (t e) -> p t e", t=TT),
                                 rb.unsqueeze(1).to_broadcast([P, TT, EXPERTS]), ALU.add))
            settle(dve)
            for t in range(TT):
                step(V.max(top8[:, 8 * t:8 * t + 8], logits[:, t, :]))
            settle(dve)
            for t in range(TT):
                step(V.max_index(idx8[:, 8 * t:8 * t + 8], top8[:, 8 * t:8 * t + 8], logits[:, t, :]))
            settle(dve)
            by8 = lambda a: a.rearrange("p (t k) -> p t k", t=TT)
            step(V.tensor_copy(idx8f, idx8))
            V.tensor_tensor(by8(gate_e), by8(top8)[:, :, 0:TOP], by8(top8)[:, :, 0:1].to_broadcast([P, TT, TOP]),
                            ALU.subtract).then_inc(S["route_act"], 1)
            settle(dve)
            hot4 = onehot.rearrange("p (t k e) -> p t k e", t=TT, k=TOP)
            hotp4 = onehot_p.rearrange("p (t k e) -> p t k e", t=TT, k=TOP)
            for t in range(TT):
                step(V.tensor_tensor(hot4[:, t], iota[:, 0:EXPERTS].unsqueeze(1).to_broadcast([P, TOP, EXPERTS]),
                                     by8(idx8f)[:, t, 0:TOP].unsqueeze(2).to_broadcast([P, TOP, EXPERTS]),
                                     ALU.is_equal))
            settle(dve)
            step(V.tensor_tensor(member, hot4[:, :, 0, :], hot4[:, :, 1, :], ALU.add))
            settle(dve)
            step(V.tensor_tensor(member, member, hot4[:, :, 2, :], ALU.add))
            settle(dve)
            V.tensor_tensor(member, member, hot4[:, :, 3, :], ALU.add).then_inc(S["route_pe"], 1)
            dve.wait_ge(S["route_pe"], 1)
            for r in range(3):
                ins = V.tensor_copy(member3[:, :, r, :], member)
                if r < 2:
                    step(ins)
            ins.then_inc(S["route_pe"], 1)
            dve.wait_ge(S["route"], 2)
            V.tensor_tensor(more[0:96, :], bank(1)[0:96, 0:1], thr[0:96, :], ALU.is_gt).then_inc(S["route_pe"], 1)
            dve.wait_ge(S["route"], 3)
            step(V.tensor_copy(more_pos, bank(2)[:, 0:1]))
            step(V.tensor_scalar(tab_n, bank(2)[0:1, 1:2], float(EXPERTS - 3), None, ALU.add))
            settle(dve)
            V.tensor_scalar(ext_hot[0:96, :], iota[0:96, 0:EXTRA], more_pos[0:96, :], more[0:96, :], ALU.is_equal,
                            ALU.mult).then_inc(S["route_pe"], 1)
            dve.wait_ge(S["route_act"], 2)
            step(V.tensor_reduce(gate_s, by8(gate_e), AX_X, ALU.add))
            settle(dve)
            step(V.reciprocal(gate_r, gate_s))
            settle(dve)
            step(V.tensor_tensor(by8(gates), by8(gate_e), gate_r.unsqueeze(2).to_broadcast([P, TT, TOP]), ALU.mult))
            settle(dve)
            for t in range(TT):
                step(V.tensor_tensor(hotp4[:, t], hot4[:, t],
                                     by8(gates)[:, t, :].unsqueeze(2).to_broadcast([P, TOP, EXPERTS]), ALU.mult))
            settle(dve)
            step(V.tensor_tensor(gate_dense, hotp4[:, :, 0, :], hotp4[:, :, 1, :], ALU.add))
            settle(dve)
            step(V.tensor_tensor(gate_dense, gate_dense, hotp4[:, :, 2, :], ALU.add))
            settle(dve)
            V.tensor_tensor(gate_dense, gate_dense, hotp4[:, :, 3, :], ALU.add).then_inc(S["route_pe"], 1)
            dve.wait_ge(S["route_pe"], 5)
            dve.wait_ge(S["route"], 5)
            step(V.tensor_copy(pos, bank(0)[:, 0:128]))
            settle(dve)
            for t in range(TT):
                step(V.tensor_tensor(hotp4[:, t], hot4[:, t],
                                     pos[:, 32 * t:32 * t + 32].unsqueeze(1).to_broadcast([P, TOP, EXPERTS]), ALU.mult))
            settle(dve)
            step(V.tensor_reduce(pos_k, onehot_p.rearrange("p (n e) -> p n e", e=EXPERTS), AX_X, ALU.add))
            settle(dve)
            step(V.tensor_scalar(hi1, pos_k, float(P), None, ALU.is_ge))
            step(V.tensor_scalar(hi2, pos_k, float(2 * P), None, ALU.is_ge))
            step(V.tensor_scalar(hi, pos_k, float(3 * P), None, ALU.is_ge))
            settle(dve)
            step(V.tensor_tensor(hi1, hi1, hi2, ALU.add))
            settle(dve)
            step(V.tensor_tensor(hi, hi, hi1, ALU.add))
            settle(dve)
            step(V.scalar_tensor_tensor(out=lo, in0=hi, scalar=-float(P), in1=pos_k, op0=ALU.mult, op1=ALU.add))
            step(V.scalar_tensor_tensor(out=by8(key), in0=by8(hi), scalar=float(EXPERTS), in1=by8(idx8f)[:, :, 0:TOP],
                                        op0=ALU.mult, op1=ALU.add))
            step(V.tensor_copy(gates_t, bank(7)[0:EXPERTS, :]))
            settle(dve)
            V.tensor_copy(tab_f[:, :, EXPERTS:BLOCKS], bank(3)[:, 0:2 * EXTRA].rearrange(
                "p (a b) -> p a b", a=2)).then_inc(S["route_pe"], 1)
            dve.wait_ge(S["route_pe"], 6)
            for n in range(TT * TOP):
                if n >= 2:
                    dve.wait_ge(S["route"], 5 + n - 1)
                one = slice(n, n + 1)
                step(V.tensor_scalar(lo_hot[:, n % 2, :], iota, lo[:, one], None, ALU.is_equal))
                step(V.tensor_scalar(key_hot[:, n % 2, 0:P], iota, key[:, one], tok_id[:, one], ALU.is_equal, ALU.mult))
                settle(dve)
                V.tensor_scalar(key_hot[:, n % 2, P:2 * P], iota, key[:, one], gates[:, one], ALU.is_equal,
                                ALU.mult).then_inc(S["route_pe"], 1)
            dve.wait_ge(S["route"], 5 + TT * TOP)
            step(V.tensor_scalar(slot_tok, bank(4)[:, 0:P], float(UNUSED), None, ALU.add))
            step(V.tensor_copy(slot_gate, bank(4)[:, P:2 * P]))
            step(V.tensor_copy(tab[:, 0:2 * BLOCKS], tab_f[0:1, :, :].rearrange("p a b -> p (a b)")))
            step(V.tensor_scalar(blk_hot, tab_f[:, 0, :], mod32, None, ALU.is_equal))
            settle(dve)
            V.tensor_copy(pos[:, 0:1], thr).then_inc(S["tables_ready"], 1)
            dve.wait_ge(S["tables_ready"], 1)
            n_more = dve.value_load(tab_n, min_val=EXPERTS - 3, max_val=MAX_BLOCKS - 3)

            def x_low(b):
                dve.wait_ge(S["x_hi_ready"], b + 1)
                V.tensor_tensor(flat(x_lo[:, :, :]), bank(6, 2), flat(x_hi[:, :, :]).bitcast(F32), ALU.subtract).then_inc(
                    S["xgt_ready"], 1)

            def a_low(b):
                dve.wait_ge(S["a_hi_ready"], b + 1)
                V.tensor_tensor(flat(a_lo[:, :, :]), bank(6, 2), flat(a_hi[:, :, :]).bitcast(F32),
                                ALU.subtract).then_inc(S["actt_ready"], 1)

            def pick(b, units):
                at_least(dve, S["w_used"], units)
                hot = blk_hot[0:96, bass.ds(b, 1)] if not isinstance(b, int) else blk_hot[0:96, b:b + 1]
                V.tensor_scalar(sel[0:96, :], tri_ones, hot, None, ALU.mult).then_inc(S["sel_ready"], 1)

            tri_ones = iota[0:96, :]

            def clip_glu(b, units):
                dve.wait_ge(S["w_used"], units)
                V.tensor_scalar(glu, bank(0, 2), LIMIT, None, ALU.min).then_inc(S["clipped"], 1)

            def clip_lin(b):
                V.tensor_scalar(lin, bank(2, 2), LIMIT, -LIMIT, ALU.min, ALU.max).then_inc(S["clipped"], 1)

            def gate_lin(b):
                dve.wait_ge(S["clipped"], 2 * b + 2)
                V.scalar_tensor_tensor(out=lin, in0=lin, scalar=1.0, in1=glu, op0=ALU.add, op1=ALU.mult).then_inc(
                    S["lin_ready"], 1)

            def times_sigmoid(b):
                dve.wait_ge(S["lin_ready"], b + 1)
                dve.wait_ge(S["sig2_ready"], b + 1)
                V.tensor_tensor(act_sb, lin, sg, ALU.mult).then_inc(S["act_ready"], 1)

            def low_in_turn(i, j):
                low(unit(i, j), (2 * UNITS_W1 + j) % RAW, j % PARTS)

            step(V.memset(iota, 1.0))
            settle(dve)
            dve.wait_ge(S["b1_ready"], 1)
            low_first(3)
            dve.wait_ge(S["rows_stored"], 16 * TT)
            x_low(0)
            pick(0, 0)
            for n in range(4, UNITS_W1):
                low_first(n)

            def first_step(b, units):
                clip_glu(b - 1, units)
                clip_lin(b - 1)

            low_first(8)
            first_step(1, UNITS_W1)
            x_low(1)
            pick(1, UNITS_W1)
            low_first(9)
            low_first(10)
            gate_lin(0)
            low_first(11)
            dve.wait_ge(S["moe_stored"], 16 * 2 * TT)
            times_sigmoid(0)
            for n in range(12, 15):
                low_first(n)
            a_low(0)
            low_first(15)

            def turn(i):
                b = i + 2
                for j in range(3):
                    low_in_turn(i, j)
                first_step(b, unit(i, 0))
                low_in_turn(i, 3)
                x_low(b)
                pick(b, unit(i, 0))
                low_in_turn(i, 4)
                gate_lin(b - 1)
                low_in_turn(i, 5)
                times_sigmoid(b - 1)
                for j in range(6, 11):
                    low_in_turn(i, j)
                a_low(b - 1)
                low_in_turn(i, 11)

            with dve.Fori(0, n_more) as i:
                turn(i)
            turn(n_more)
            low_in_turn(n_more + 1, 0)
            first_step(n_more + 3, unit(n_more + 1, 0))
            gate_lin(n_more + 2)
            low_in_turn(n_more + 1, 1)
            times_sigmoid(n_more + 2)
            for j in range(2, 5):
                low_in_turn(n_more + 1, j)
            a_low(n_more + 2)
            for j in range(5, 8):
                low_in_turn(n_more + 1, j)

            def normed(t):
                rms_factor(rstd[:, t:t + 1], ssq[:, t:t + 1], 11 + t)
                V.scalar_tensor_tensor(out=x_sb[:, t], in0=x_sb[:, t], scalar=rstd[:, t:t + 1], in1=fnw,
                                       op0=ALU.mult, op1=ALU.mult).then_inc(S["out_ready"], 1)

            dve.wait_ge(S["fnw_landed"], 16)
            for t in range(TT):
                dve.wait_ge(moe_landed[t], 16)
                step(V.tensor_tensor(xh[:, t], xh[:, t], g2_b[:, :], ALU.mult))
                settle(dve)
                V.tensor_tensor(x_sb[:, t], x_sb[:, t], xh[:, t], ALU.add).then_inc(S["fin"], 1)
                if t >= 1:
                    normed(t - 1)
            normed(TT - 1)


_INS = ['x', 'c', 'ada_w', 'ada_b', 'norm1_w', 'w_in', 'hg_lb_logits', 'hg_norm_w', 'ssm_a_log', 'ssm_dt_bias',
        'ssm_d', 'ssm_conv_w', 'ssm_conv_b', 'ssm_norm_w', 'w_out', 'norm2_w', 'router_w', 'router_b',
        'exp_w1', 'exp_b1', 'exp_w2', 'exp_b2', 'final_norm_w']
_OUTS = [((1, 512, 1024), 'float32')]


def kernel(**inputs):
    import numpy as _np
    import concourse.bacc as _bacc
    from concourse import mybir as _mybir
    from concourse.bass_utils import run_bass_kernel_spmd as _run

    nc = _bacc.Bacc("TRN2", target_bir_lowering=False, num_devices=1)
    arrays, args = {}, []
    for name in _INS:
        a = _np.ascontiguousarray(inputs[name])
        arrays[f"in_{name}_dram"] = a
        args.append(nc.dram_tensor(f"in_{name}_dram", a.shape, _mybir.dt.from_np(a.dtype), kind="ExternalInput").ap())
    for i, (shape, dtype) in enumerate(_OUTS):
        dt = _mybir.dt.from_np(_np.dtype(dtype))
        args.append(nc.dram_tensor(f"out_{i}_dram", shape, dt, kind="ExternalOutput").ap())
    build(nc, *args)
    r = _run(nc, [arrays], core_ids=[0])
    got = tuple(r.results[0][f"out_{i}_dram"] for i in range(len(_OUTS)))
    return got[0]
```
